# Optimizing a Trainium2 kernel written in Bass

```python
import jax, jax.numpy as jnp
from jax import lax
import numpy as np

D_MODEL = 1024
BATCH = 1
SEQ = 2048
DEPTH = 1

MEM_LEN = 256
CHUNK = 64
EPS = 1e-6
MLSTM_HEADS = 4
MLSTM_W = D_MODEL // 2
MLSTM_HD = MLSTM_W // MLSTM_HEADS
CONV_W = 4
F_BIAS_LO = 3.0
F_BIAS_HI = 6.0
GLA_HEADS = 4
GLA_WV = D_MODEL // 2
GLA_WK = GLA_WV // 2
GLA_DK = GLA_WK // GLA_HEADS
GLA_DV = GLA_WV // GLA_HEADS
GLA_RANK = 16
GLA_TAU = 16.0
XATTN_HEADS = 4
XATTN_HD = D_MODEL // XATTN_HEADS
D_FF = 4 * D_MODEL

IN_SPLITS = [MLSTM_W, MLSTM_W, MLSTM_W, MLSTM_W, MLSTM_HEADS, MLSTM_HEADS,
             GLA_WK, GLA_WK, GLA_WV, GLA_WV, GLA_RANK]
D_IN = sum(IN_SPLITS)
IN_SPLIT_IDX = [int(c) for c in np.cumsum(IN_SPLITS)[:-1]]
MIX_W = MLSTM_W + GLA_WV

kernel_name = 'hybrid_mlstm_gla_block'

def rmsnorm(x, g):
    xf = x.astype(jnp.float32)
    y = xf * lax.rsqrt(jnp.mean(xf * xf, axis=-1, keepdims=True) + EPS)
    return y.astype(x.dtype) * g

def head_rmsnorm(h, g):
    y = h * lax.rsqrt(jnp.mean(h * h, axis=-1, keepdims=True) + EPS)
    B, S = y.shape[:2]
    return y.reshape(B, S, -1) * g.astype(jnp.float32)

def causal_conv(x, w, b):
    S = x.shape[1]
    xp = jnp.pad(x, ((0, 0), (CONV_W - 1, 0), (0, 0)))
    y = xp[:, 0:S] * w[0]
    for j in range(1, CONV_W):
        y = y + xp[:, j:j + S] * w[j]
    return y + b

def to_chunks(t, n_heads):
    B, S = t.shape[:2]
    return t.reshape(B, S // CHUNK, CHUNK, n_heads, -1).transpose(1, 0, 3, 2, 4)

def gate_chunks(t):
    B, S, H = t.shape
    return t.reshape(B, S // CHUNK, CHUNK, H).transpose(1, 0, 3, 2)

def from_chunks(t):
    NC, B, H, L, d = t.shape
    return t.transpose(1, 0, 3, 2, 4).reshape(B, NC * L, H, d)

def mlstm_chunkwise(q, k, v, log_i, log_f):
    NC, B, H, L, d = q.shape
    causal = jnp.tril(jnp.ones((L, L), dtype=bool))

    def step(carry, inp):
        C, n, m = carry
        qc, kc, vc, li, lf = inp
        b = jnp.cumsum(lf, axis=-1)
        D = jnp.where(causal, b[..., :, None] - b[..., None, :] + li[..., None, :], -jnp.inf)
        inter = b + m[..., None]
        m_t = jnp.maximum(jnp.max(D, axis=-1), inter)
        s = jnp.einsum('bhtd,bhsd->bhts', qc, kc) * jnp.exp(D - m_t[..., None])
        w_inter = jnp.exp(inter - m_t)
        num = (jnp.einsum('bhts,bhse->bhte', s, vc)
               + w_inter[..., None] * jnp.einsum('bhtd,bhde->bhte', qc, C))
        den = jnp.sum(s, axis=-1) + w_inter * jnp.einsum('bhtd,bhd->bht', qc, n)
        h = num / jnp.maximum(jnp.abs(den), jnp.exp(-m_t))[..., None]
        bL = b[..., -1]
        g = bL[..., None] - b + li
        m_new = jnp.maximum(bL + m, jnp.max(g, axis=-1))
        decay = jnp.exp(bL + m - m_new)
        wk = jnp.exp(g - m_new[..., None])[..., None] * kc
        C_new = decay[..., None, None] * C + jnp.einsum('bhsd,bhse->bhde', wk, vc)
        n_new = decay[..., None] * n + jnp.sum(wk, axis=2)
        return (C_new, n_new, m_new), h

    init = (jnp.zeros((B, H, d, v.shape[-1]), jnp.float32),
            jnp.zeros((B, H, d), jnp.float32),
            jnp.zeros((B, H), jnp.float32))
    _, h = lax.scan(step, init, (q, k, v, log_i, log_f))
    return h

def gla_chunkwise(q, k, v, log_a):
    NC, B, H, L, dk = q.shape
    causal = jnp.tril(jnp.ones((L, L), dtype=bool))

    def step(Sst, inp):
        qc, kc, vc, la = inp
        b = jnp.cumsum(la, axis=2)
        diff = jnp.where(causal[:, :, None], b[:, :, :, None, :] - b[:, :, None, :, :], -jnp.inf)
        A = jnp.einsum('bhtd,bhsd,bhtsd->bhts', qc, kc, jnp.exp(diff))
        o = (jnp.einsum('bhts,bhse->bhte', A, vc)
             + jnp.einsum('bhtd,bhde->bhte', qc * jnp.exp(b), Sst))
        bL = b[:, :, -1]
        kw = kc * jnp.exp(bL[:, :, None] - b)
        S_new = jnp.exp(bL)[..., None] * Sst + jnp.einsum('bhsd,bhse->bhde', kw, vc)
        return S_new, o

    init = jnp.zeros((B, H, dk, v.shape[-1]), jnp.float32)
    _, o = lax.scan(step, init, (q, k, v, log_a))
    return o

def setup_inputs(seed: int = 0) -> dict:
    key = jax.random.key(seed)
    ks = jax.random.split(key, 24)
    f32 = jnp.float32

    def nrm(k, shape, scale):
        return jax.random.normal(k, shape, f32) * scale

    def gain(k, shape):
        return 1.0 + 0.01 * jax.random.normal(k, shape, f32)

    f_bias = (jnp.linspace(F_BIAS_LO, F_BIAS_HI, MLSTM_HEADS, dtype=f32)[None]
              + nrm(ks[6], (DEPTH, MLSTM_HEADS), 0.01))
    return {
        'x': nrm(ks[0], (BATCH, SEQ, D_MODEL), 1.0),
        'mem': nrm(ks[1], (BATCH, MEM_LEN, D_MODEL), 1.0),
        'mix_norm_g': gain(ks[2], (DEPTH, D_MODEL)),
        'w_in': nrm(ks[3], (DEPTH, D_MODEL, D_IN), D_MODEL ** -0.5),
        'conv_w': nrm(ks[4], (DEPTH, CONV_W, 2 * MLSTM_W), CONV_W ** -0.5),
        'conv_b': nrm(ks[5], (DEPTH, 2 * MLSTM_W), 0.01),
        'mlstm_i_b': nrm(ks[7], (DEPTH, MLSTM_HEADS), 0.1),
        'mlstm_f_b': f_bias,
        'mlstm_norm_g': gain(ks[8], (DEPTH, MLSTM_W)),
        'gla_wa2': nrm(ks[9], (DEPTH, GLA_RANK, GLA_WK), GLA_RANK ** -0.5),
        'gla_ba': nrm(ks[10], (DEPTH, GLA_WK), 0.1),
        'gla_norm_g': gain(ks[11], (DEPTH, GLA_WV)),
        'w_out': nrm(ks[12], (DEPTH, MIX_W, D_MODEL), MIX_W ** -0.5),
        'xattn_norm_g': gain(ks[13], (DEPTH, D_MODEL)),
        'mem_norm_g': gain(ks[14], (DEPTH, D_MODEL)),
        'wq_x': nrm(ks[15], (DEPTH, D_MODEL, D_MODEL), D_MODEL ** -0.5),
        'wk_x': nrm(ks[16], (DEPTH, D_MODEL, D_MODEL), D_MODEL ** -0.5),
        'wv_x': nrm(ks[17], (DEPTH, D_MODEL, D_MODEL), D_MODEL ** -0.5),
        'wo_x': nrm(ks[18], (DEPTH, D_MODEL, D_MODEL), D_MODEL ** -0.5),
        'mlp_norm_g': gain(ks[19], (DEPTH, D_MODEL)),
        'w1': nrm(ks[20], (DEPTH, D_MODEL, D_FF), D_MODEL ** -0.5),
        'w2': nrm(ks[21], (DEPTH, D_FF, D_MODEL), D_FF ** -0.5),
        'final_norm_g': gain(ks[22], (D_MODEL,)),
    }

def reference(x, mem, mix_norm_g, w_in, conv_w, conv_b, mlstm_i_b, mlstm_f_b, mlstm_norm_g,
              gla_wa2, gla_ba, gla_norm_g, w_out, xattn_norm_g, mem_norm_g, wq_x, wk_x, wv_x,
              wo_x, mlp_norm_g, w1, w2, final_norm_g):
    f32 = jnp.float32
    dt = x.dtype
    B, S, _ = x.shape
    M = mem.shape[1]
    for l in range(DEPTH):
        h = rmsnorm(x, mix_norm_g[l])
        u = h @ w_in[l]
        mq, mk, mv, mo, mi, mf, gq, gk, gv, gr, ga = jnp.split(u, IN_SPLIT_IDX, axis=-1)

        qk = jax.nn.silu(causal_conv(jnp.concatenate([mq, mk], axis=-1), conv_w[l], conv_b[l]))
        mq, mk = jnp.split(qk, 2, axis=-1)
        log_i = (mi + mlstm_i_b[l]).astype(f32)
        log_f = jax.nn.log_sigmoid((mf + mlstm_f_b[l]).astype(f32))
        h_m = mlstm_chunkwise(to_chunks((mq * MLSTM_HD ** -0.5).astype(f32), MLSTM_HEADS),
                              to_chunks(mk.astype(f32), MLSTM_HEADS),
                              to_chunks(mv.astype(f32), MLSTM_HEADS),
                              gate_chunks(log_i), gate_chunks(log_f))
        h_m = head_rmsnorm(from_chunks(h_m), mlstm_norm_g[l]).astype(dt) * jax.nn.sigmoid(mo)

        log_a = jax.nn.log_sigmoid((ga @ gla_wa2[l] + gla_ba[l]).astype(f32)) / GLA_TAU
        h_g = gla_chunkwise(to_chunks((gq * GLA_DK ** -0.5).astype(f32), GLA_HEADS),
                            to_chunks(gk.astype(f32), GLA_HEADS),
                            to_chunks(gv.astype(f32), GLA_HEADS),
                            to_chunks(log_a, GLA_HEADS))
        h_g = head_rmsnorm(from_chunks(h_g), gla_norm_g[l]).astype(dt) * jax.nn.silu(gr)

        x = x + jnp.concatenate([h_m, h_g], axis=-1) @ w_out[l]

        hq = (rmsnorm(x, xattn_norm_g[l]) @ wq_x[l]).reshape(B, S, XATTN_HEADS, XATTN_HD)
        mn = rmsnorm(mem, mem_norm_g[l])
        mk_ = (mn @ wk_x[l]).reshape(B, M, XATTN_HEADS, XATTN_HD)
        mv_ = (mn @ wv_x[l]).reshape(B, M, XATTN_HEADS, XATTN_HD)
        scores = jnp.einsum('bshd,bmhd->bhsm', hq, mk_).astype(f32) * (XATTN_HD ** -0.5)
        p = jax.nn.softmax(scores, axis=-1).astype(dt)
        att = jnp.einsum('bhsm,bmhd->bshd', p, mv_).reshape(B, S, D_MODEL)
        x = x + att @ wo_x[l]

        hm = rmsnorm(x, mlp_norm_g[l]) @ w1[l]
        x = x + jnp.square(jax.nn.relu(hm)) @ w2[l]
    return rmsnorm(x, final_norm_g)


_drawn_inputs = setup_inputs


def setup_inputs(seed=0):
    import zlib

    import numpy as np

    out = dict(_drawn_inputs(seed))
    spreads = {}
    factors = {'mix_norm_g': 5.368,
     'conv_b': 64.0,
     'mlstm_i_b': 64.0,
     'mlstm_norm_g': 200.0,
     'gla_ba': 3.067,
     'gla_norm_g': 35.018,
     'xattn_norm_g': 23.447,
     'mem_norm_g': 24.349,
     'mlp_norm_g': 177.225,
     'final_norm_g': 178.351}
    for name, (base, spread) in spreads.items():
        noise = np.random.default_rng([zlib.crc32(name.encode()), seed]).standard_normal(out[name].shape)
        drawn = base * np.exp(spread * noise) if base else spread * noise
        out[name] = __import__('jax').numpy.asarray(drawn.astype(out[name].dtype))
    for name, factor in factors.items():
        out[name] = (out[name] * factor).astype(out[name].dtype)
    return out
```

```python
from contextlib import ExitStack

import numpy as np

import concourse.bass as bass
from concourse import mybir

F32 = mybir.dt.float32
F32R = mybir.dt.float32r
ACT = mybir.ActivationFunctionType
ALU = mybir.AluOpType
AX = mybir.AxisListType

P = 128
D = 1024
SEQ = 2048
GROUP = 512
CH = 128
NCH = GROUP // CH
NG = SEQ // GROUP
MEM = 256
KT = D // P
COLS = 512
HEADS = 4
HD = 128
DK = 64
XHD = 256
FF = 4096
CONV = 4
RANK = 16
EPS = 1e-6
BIG = 1e30
TAU = 16.0

C_MQ, C_MK, C_MV, C_MO = 0, 512, 1024, 1536
C_MI = 2048
C_GQ = 2056
C_GV = 2568
C_GR = 3080
C_GA = 3592
NGATE = 2 * HEADS + RANK

RING = 4
LEAD = 3
PAIRS = 4

B_MQ, B_MK, B_MO, B_GR, B_MV, B_GQK, B_GV, B_OUT, B_Q, B_O, B_MLP = 0, 1, 2, 3, 4, 5, 6, 7, 9, 11, 13
HB = FF // D
GROUP_SLABS = (B_MLP + 4 * HB) * KT
PRO_SLABS = 4 * KT
GROUP_BANKS = 4 * (B_MLP + 4 * HB + 2)
PRO_BANKS = 12
U_OUT, U_Q, U_PV, U_O, U_MLP = 28, 36, 44, 52, 60

TRS = 32
LEVELS = 7
NORMS = 4


def program(nc, A, out):
    ctx = ExitStack()
    with ctx:
        def sb(name, shape, dt=F32, stack=None):
            return (stack or ctx).enter_context(nc.sbuf_tensor(name, shape, dt))

        def sem(name):
            return ctx.enter_context(nc.semaphore(name))

        ident = sb("ident", [P, P])
        ones16 = sb("ones16", [16, P])
        causal = sb("causal", [P, P])
        lvl_mask = sb("lvl_mask", [P, 7, 64])
        norm_g = sb("norm_g", [P, 4, KT])
        conv_w = sb("conv_w", [P, CONV, KT])
        conv_b = sb("conv_b", [P, KT])
        gate_b = sb("gate_b", [16, 2])
        wa2 = sb("wa2", [RANK, 256])
        ba = sb("ba", [P, 2])
        wg_raw = sb("wg_raw", [P, KT, NGATE])
        wg_hi = sb("wg_hi", [P, KT, NGATE], F32R)
        wg_lo = sb("wg_lo", [P, KT, NGATE], F32R)

        xres = sb("xres", [P, NCH, D])
        tok = sb("tok", [P, NCH, D])
        act_hi = sb("act_hi", [P, KT, GROUP], F32R)
        act_lo = sb("act_lo", [P, KT, GROUP], F32R)
        raw = sb("raw", [P, PAIRS, 2, COLS])
        w_hi = sb("w_hi", [P, RING, COLS], F32R)
        w_lo = sb("w_lo", [P, RING, COLS], F32R)
        memK = sb("memK", [P, KT, MEM])
        memV = sb("memV", [P, 2, D])
        qk = sb("qk", [P, KT, GROUP])
        halo = sb("halo", [P, KT, CONV - 1])
        stC = sb("stC", [P, HEADS, HD + 1])
        stS = sb("stS", [P, 2, HD])
        mrow = sb("mrow", [1, NCH + 1, HEADS])
        ss = sb("ss", [P, NCH])
        var = sb("var", [P, NCH])
        lnv = sb("lnv", [P, NCH])
        y0 = sb("y0", [P, NCH])
        y1 = sb("y1", [P, NCH])
        rstd = sb("rstd", [P, NCH])
        hss = sb("hss", [P, 2, NCH, HEADS])
        hinv = sb("hinv", [P, NCH, HEADS])
        hden = sb("hden", [P, NCH, HEADS])
        hvar = sb("hvar", [P, 2, NCH, HEADS])
        hln = sb("hln", [P, 2, NCH, HEADS])
        hy0 = sb("hy0", [P, 2, NCH, HEADS])
        hy1 = sb("hy1", [P, 2, NCH, HEADS])
        hscale = sb("hscale", [P, 2, NCH, HEADS])

        mixing = ExitStack()
        vext = sb("vext", [P, NCH, HEADS, HD + 1], F32, mixing)
        gqk = sb("gqk", [P, 4, GROUP], F32, mixing)
        gv = sb("gv", [P, NCH, COLS], F32, mixing)
        decay = sb("decay", [P, 2, GROUP], F32, mixing)
        zz = sb("zz", [P, 2 * LEVELS * 256], F32, mixing)
        Z = zz[:, :].rearrange("p (b l n) -> p b l n", b=2, l=LEVELS)
        ubuf = zz[:, 0:4 * (GROUP + 3)].rearrange("p (i n) -> p i n", i=4)
        zmin = zz[:, 4 * (GROUP + 3):4 * (GROUP + 3) + 2 * GROUP].rearrange("p (j n) -> p j n", j=2)
        sg = sb("sg", [P, 2, COLS], F32, mixing)
        gif = sb("gif", [P, 2, NCH, HEADS], F32, mixing)
        gga = sb("gga", [P, NCH, RANK], F32, mixing)
        rows = sb("rows", [16, 8, CH], F32, mixing)
        R_LI, R_LF, R_B, R_A, R_M, R_P, R_WK, R_EM = range(8)
        rtmp = sb("rtmp", [16, 2, CH], F32, mixing)
        gaT = sb("gaT", [RANK, GROUP], F32, mixing)
        rcol = sb("rcol", [16, 3], F32, mixing)
        mlast = sb("mlast", [1, 2, 16], F32, mixing)
        diag = sb("diag", [16, 2, 16], F32, mixing)
        bc = sb("bc", [P, 2, 16], F32, mixing)
        cols = sb("cols", [P, 3, 16], F32, mixing)
        pdiag = gaT[:].rearrange("p (h t) -> p h t", h=HEADS)
        mw = sb("mw", [P, 3 * COLS], F32, mixing)
        ew, arg, wk = (mw[:, k * COLS:(k + 1) * COLS].rearrange("p (h t) -> p h t", h=HEADS) for k in range(3))
        qw, sm = (sg[:, k, :].rearrange("p (h t) -> p h t", h=HEADS) for k in range(2))
        msk = mw[:, 0:2 * 448].rearrange("p (b l t) -> p b l t", b=2, l=7)
        ad = mw[:, 896:1152].rearrange("p (h t) -> p h t", h=HEADS)
        a2 = mw[0:64, 1152:1408].rearrange("p (h t) -> p h t", h=HEADS)
        head_g = sb("head_g", [P, D], F32, mixing)
        eb = head_g[:, 0:COLS].rearrange("p (b j t) -> p b j t", b=2, j=2)
        ekw = head_g[:, COLS:].rearrange("p (b j t) -> p b j t", b=2, j=2)
        bend = sb("bend", [P, 2, 2], F32, mixing)
        qe = sb("qe", [P, 2, 2, CH], F32, mixing)
        kwT = sb("kwT", [P, 2 * CH], F32, mixing)
        mixing.close()
        later = ExitStack()
        h_hi = sb("h_hi", [P, KT, GROUP], F32R, later)
        h_lo = sb("h_lo", [P, KT, GROUP], F32R, later)
        hr = sb("hr", [P, 4, GROUP], F32, later)
        hsq = sb("hsq", [P, 2, GROUP], F32, later)
        fin_g = sb("fin_g", [P, D], F32, later)
        later.close()
        attn = ExitStack()
        pr = sb("pr", [P, 2, HEADS, MEM], F32, attn)
        prT = sb("prT", [P, HEADS, 2, GROUP], F32, attn)
        smax = sb("smax", [P, 2, HEADS], F32, attn)
        ssum = sb("ssum", [P, 2, HEADS], F32, attn)
        sinv = sb("sinv", [P, 2, HEADS], F32, attn)
        attn.close()

        bank = [ctx.enter_context(nc.psum_tensor(f"bank{i}", [P, 512], F32)) for i in range(4)]
        work = ctx.enter_context(nc.psum_tensor("work", [P, 4, 512], F32))

        const_in = sem("const_in")
        const_made = sem("const_made")
        gate_w_hi = sem("gate_w_hi")
        gate_w_lo = sem("gate_w_lo")
        x_in = sem("x_in")
        pair_in = [sem(f"pair_in{i}") for i in range(PAIRS)]
        slab_hi = sem("slab_hi")
        slab_lo = sem("slab_lo")
        slab_used = sem("slab_used")
        bank_full = sem("bank_full")
        bank_free = sem("bank_free")
        act_step = sem("act_step")
        dve_step = sem("dve_step")
        pe_step = sem("pe_step")
        pool_step = sem("pool_step")
        norm_ss = sem("norm_ss")
        norm_var = sem("norm_var")
        norm_guess = sem("norm_guess")
        tok_ready = sem("tok_ready")
        tr_full = sem("tr_full")
        act_hi_ready = sem("act_hi_ready")
        act_lo_ready = sem("act_lo_ready")
        gates_full = sem("gates_full")
        gates_out = sem("gates_out")
        grow_full = sem("grow_full")
        grow_out = sem("grow_out")
        la_full = sem("la_full")
        la_abs = sem("la_abs")
        la_min = sem("la_min")
        la_log = sem("la_log")
        row_log = sem("row_log")
        row_scan = sem("row_scan")
        mlast_full = sem("mlast_full")
        mrow_ready = sem("mrow_ready")
        mcol_full = sem("mcol_full")
        row_p = sem("row_p")
        row_exp = sem("row_exp")
        diag_ready = sem("diag_ready")
        cols_full = sem("cols_full")
        cols_ready = sem("cols_ready")
        conv_done = sem("conv_done")
        conv_sig = sem("conv_sig")
        qk_ready = sem("qk_ready")
        og_scaled = sem("og_scaled")
        gr_sig = sem("gr_sig")
        pdiag_ready = sem("pdiag_ready")
        ps_full = sem("ps_full")
        m_arg = sem("m_arg")
        m_exp = sem("m_exp")
        m_in = sem("m_in")
        kt_full = sem("kt_full")
        wk_ready = sem("wk_ready")
        num_full = sem("num_full")
        num_ss = sem("num_ss")
        num_out = sem("num_out")
        c_full = sem("c_full")
        c_ready = sem("c_ready")
        gla_in = sem("gla_in")
        z_diff = sem("z_diff")
        z_abs = sem("z_abs")
        z_exp = sem("z_exp")
        z_ready = sem("z_ready")
        bend_ready = sem("bend_ready")
        ekw_ready = sem("ekw_ready")
        lvl_full = sem("lvl_full")
        lvl_masked = sem("lvl_masked")
        ad_ready = sem("ad_ready")
        side_full = sem("side_full")
        side_out = sem("side_out")
        o_full = sem("o_full")
        o_ss = sem("o_ss")
        o_out = sem("o_out")
        s_full = sem("s_full")
        s_ready = sem("s_ready")
        h_var = sem("h_var")
        h_guess = sem("h_guess")
        mixed = sem("mixed")
        sc_full = sem("sc_full")
        sc_max = sem("sc_max")
        sc_exp = sem("sc_exp")
        pr_ready = sem("pr_ready")
        prT_full = sem("prT_full")
        prT_out = sem("prT_out")
        sq_hi = sem("sq_hi")
        h_sq = sem("h_sq")
        h_ready = sem("h_ready")
        v_ones = sem("v_ones")
        carrier = sem("carrier")
        av_hi = sem("av_hi")
        head_g_in = sem("head_g_in")
        fin_g_in = sem("fin_g_in")
        kq_ready = sem("kq_ready")
        stored = sem("stored")

        block = ctx.enter_context(nc.Block())

        def slab_no(g, s):
            return PRO_SLABS + GROUP_SLABS * g + s

        def use_no(g, u):
            return PRO_BANKS + GROUP_BANKS * g + u

        def read_out(eng, g, u, more=0):
            eng.wait_ge(bank_free, use_no(g, u + 1) + more)

        def stand_alone(eng):
            eng.sem_inc(carrier, 1)

        def own_results(eng, signal, base, per):
            n, group = 0, None

            def mark(ins):
                nonlocal n
                ins.then_inc(signal, 1)
                n += 1

            def settle():
                eng.wait_ge(signal, n if group is None else base + per * group + n)

            def start_group(g):
                nonlocal n, group
                assert n == base, (n, base)
                n, group = 0, g

            def end_group():
                assert n == per, (n, per)

            return mark, settle, start_group, end_group

        @block.sync
        def _(sp):
            def load_pair(slot, seen, src):
                sp.dma_start(raw[:, slot], src).then_inc(pair_in[slot], 16)

            def pair_of(w, row, col):
                return w[row:row + 2 * P, col:col + COLS].rearrange("(k p) n -> p k n", p=P)

            q = 0
            for w, col in ((A["wk_x"], 0), (A["wk_x"], COLS), (A["wv_x"], 0), (A["wv_x"], COLS)):
                for kp in range(KT // 2):
                    if q >= PAIRS:
                        sp.wait_ge(slab_lo, 2 * (q - PAIRS + 1))
                    load_pair(q % PAIRS, q, pair_of(w, kp * 2 * P, col))
                    q += 1

            fixed = [(A["w_in"], c) for c in (C_MQ, C_MK, C_MO, C_GR, C_MV, C_GQ, C_GV)]
            fixed += [(A["w_out"], 0), (A["w_out"], COLS), (A["wq_x"], 0), (A["wq_x"], COLS),
                      (A["wo_x"], 0), (A["wo_x"], COLS)]

            def load_slab_pair(n0, kp, src):
                sp.wait_ge(slab_lo, n0 + 2 * kp + 2 - 2 * PAIRS)
                load_pair(kp % PAIRS, None, src)

            with sp.Fori(0, NG) as g:
                for b, (w, col) in enumerate(fixed):
                    for kp in range(KT // 2):
                        load_slab_pair(slab_no(g, KT * b), kp, pair_of(w, kp * 2 * P, col))
                with sp.Fori(0, HB) as hb:
                    first = slab_no(g, KT * B_MLP) + 4 * KT * hb
                    for b in range(2):
                        for kp in range(KT // 2):
                            load_slab_pair(first + KT * b, kp,
                                           A["w1"][kp * 2 * P:(kp + 1) * 2 * P, bass.ds(hb * D + b * COLS, COLS)]
                                           .rearrange("(k p) n -> p k n", p=P))
                    for b in range(2):
                        for kp in range(KT // 2):
                            load_slab_pair(first + KT * (2 + b), kp,
                                           A["w2"][bass.ds(hb * D + kp * 2 * P, 2 * P), b * COLS:(b + 1) * COLS]
                                           .rearrange("(k p) n -> p k n", p=P))
            for kp in range((LEAD + 1) // 2):
                load_slab_pair(slab_no(NG, 0), kp, pair_of(A["w_in"], kp * 2 * P, C_MQ))

        @block.gpsimd
        def _(pool):
            mark, settle, start_group, end_group = own_results(pool, pool_step, POOL_BASE, POOL_PER)

            def made(ins):
                mark(ins)
                settle()

            def select(view, pattern, base, cm, fill, op=ALU.is_ge):
                made(nc.gpsimd.affine_select(out=view, in_=view, compare_op=op, fill=fill, base=base,
                                             pattern=pattern, channel_multiplier=cm))

            made(nc.gpsimd.memset(ident[:], 0.0))
            select(ident[:], [[-1, P]], 0, 1, 1.0, ALU.not_equal)
            made(nc.gpsimd.memset(ones16[:], 1.0))
            made(nc.gpsimd.memset(causal[:], 0.0))
            select(causal[:], [[1, P]], 0, -1, BIG)
            tmp = tok[:, 0, 0:P]
            for lv in range(6):
                half = 32 >> lv
                nb = P // (2 * half)
                tv = tmp.rearrange("p (b r h) -> p b r h", r=2, h=half)
                made(nc.gpsimd.memset(tmp, 0.0))
                made(nc.gpsimd.memset(tv[:, :, 1, :], 1.0))
                select(tmp, [[-2 * half, nb], [0, 2 * half]], 0, 1, 0.0)
                select(tmp, [[2 * half, nb], [0, 2 * half]], half - 1, -1, 0.0)
                made(nc.gpsimd.tensor_copy(lvl_mask[0:64, lv, :], tmp[0:64, 0:64]))
                made(nc.gpsimd.tensor_copy(lvl_mask[64:128, lv, :], tmp[64:128, 64:128]))
            made(nc.gpsimd.tensor_copy(lvl_mask[0:64, 6, :], ident[0:64, 0:64]))
            made(nc.gpsimd.tensor_copy(lvl_mask[64:128, 6, :], ident[64:128, 64:128]))
            made(nc.gpsimd.memset(stC[:], 0.0))
            made(nc.gpsimd.memset(stS[:], 0.0))
            made(nc.gpsimd.memset(halo[:], 0.0))
            made(nc.gpsimd.memset(mrow[0:1, 1:NCH + 1, :], 0.0))
            nc.gpsimd.memset(mrow[0:1, 0, :], 0.0).then_inc(const_made, 1)

            pool.wait_ge(tok_ready, 2)
            with pool.Fori(0, NG) as g:
                start_group(g)
                stand_alone(pool)
                for i in range(NCH):
                    pool.dma_start(xres[:, i, :], A["x"][bass.ds(g * GROUP + i * P, P), :]).then_inc(x_in, 16)
                pool.dma_start(head_g[:, 0:COLS], A["mlstm_norm_g"].partition_broadcast(P)).then_inc(head_g_in, 16)
                pool.dma_start(head_g[:, COLS:], A["gla_norm_g"].partition_broadcast(P)).then_inc(head_g_in, 16)
                pool.wait_ge(head_g_in, 32 * (g + 1))
                for half in range(2):
                    for i in range(NCH):
                        read_out(pool, g, 4 * (B_MO + half) + i)
                        v = tok[:, i, half * COLS:(half + 1) * COLS]
                        nc.gpsimd.tensor_tensor(v, v, head_g[:, half * COLS:(half + 1) * COLS],
                                                ALU.mult).then_inc(og_scaled, 1)
                def distances(c):
                    t0 = c * CH
                    if c == 0:
                        pool.wait_ge(gla_in, g + 1)
                    if c >= 2:
                        pool.wait_ge(lvl_full, 16 * g + 4 * (c - 1))
                    for lv in range(LEVELS):
                        half = 64 >> lv
                        v = Z[:, c % 2, lv, :].rearrange("p (j b n) -> p j b n", j=2, n=2 * half)
                        src = decay[:, :, t0:t0 + CH].rearrange("p j (b n) -> p j b n", n=2 * half)
                        mid = src[:, :, :, half - 1:half].to_broadcast(list(src.shape))
                        ins = nc.gpsimd.tensor_tensor(v, src, mid, ALU.subtract)
                    ins.then_inc(z_diff, 1)

                def products(c):
                    t0 = c * CH
                    if c == 0:
                        read_out(pool, g, 4 * B_GQK + 3)
                    pool.wait_ge(z_exp, 4 * g + c + 1)
                    for lv in range(LEVELS):
                        half = 64 >> lv
                        v = Z[:, c % 2, lv, :].rearrange("p (j b r n) -> p j b r n", j=2, r=2, n=half)
                        for r, tile in ((0, 2), (1, 0)):
                            src = gqk[:, tile:tile + 2, t0:t0 + CH].rearrange(
                                "p j (b r n) -> p j b r n", r=2, n=half)[:, :, :, r, :]
                            ins = nc.gpsimd.tensor_tensor(v[:, :, :, r, :], v[:, :, :, r, :], src, ALU.mult)
                    ins.then_inc(z_ready, 1)

                distances(0)
                distances(1)
                products(0)
                products(1)
                for c in range(2, NCH):
                    distances(c)
                    products(c)
                pool.wait_ge(mixed, 2 * g + 2)
                stand_alone(pool)
                pool.dma_start(fin_g[:], A["final_norm_g"].partition_broadcast(P)).then_inc(fin_g_in, 16)
                pool.wait_ge(fin_g_in, 16 * (g + 1))
                for i in range(NCH):
                    pool.wait_ge(tok_ready, 2 + 16 * g + 12 + i + 1)
                    mark(nc.gpsimd.tensor_tensor(tok[:, i, :], tok[:, i, :], fin_g[:], ALU.mult))
                    settle()
                    stand_alone(pool)
                    pool.dma_start(out[bass.ds(g * GROUP + i * P, P), :], tok[:, i, :]).then_inc(stored, 16)
                end_group()
                pool.wait_ge(stored, 16 * NCH * (g + 1))

        @block.scalar
        def _(act):
            mark, settle, start_group, end_group = own_results(act, act_step, ACT_BASE, ACT_PER)
            n_const = 0
            for dst, src in ((norm_g[:, 0, :], A["mix_norm_g"]),
                             (norm_g[:, 1, :], A["xattn_norm_g"]),
                             (norm_g[:, 2, :], A["mlp_norm_g"]),
                             (norm_g[:, 3, :], A["mem_norm_g"]),
                             (xres[:, 0, :], A["mem"][0:P, :]), (xres[:, 1, :], A["mem"][P:2 * P, :]),
                             (conv_b[:, :], A["conv_b"]),
                             (conv_w[:, :, :], A["conv_w"]),
                             (wa2[:, :], A["gla_wa2"]),
                             (ba[:, :], A["gla_ba"]),
                             (wg_raw[:, :, 0:2 * HEADS],
                              A["w_in"][:, C_MI:C_MI + 2 * HEADS].rearrange("(k p) n -> p k n", p=P)),
                             (wg_raw[:, :, 2 * HEADS:],
                              A["w_in"][:, C_GA:C_GA + RANK].rearrange("(k p) n -> p k n", p=P))                             ):
                act.dma_start(dst, src).then_inc(const_in, 16)
                n_const += 1
            for c in range(NCH):
                for k, name in enumerate(("mlstm_i_b", "mlstm_f_b")):
                    act.dma_start(gate_b[c * HEADS:(c + 1) * HEADS, k:k + 1],
                                  A[name].rearrange("(h o) -> h o", o=1)).then_inc(const_in, 16)
                    n_const += 1
            assert n_const == N_CONST

            nc.scalar.preload_act_table_set("natural_log_exp_and_others")

            def split_hi(slot, pair_slot, pair_count, use):
                if pair_count is not None:
                    act.wait_ge(pair_in[pair_slot], 16 * pair_count)
                if use is not None:
                    act.wait_ge(*use)
                nc.scalar.activation(w_hi[:, slot, :], raw[:, pair_slot, slot % 2, :], ACT.Copy).then_inc(slab_hi, 1)

            def split_pro(n):
                m = n - RING
                b, kt = divmod(m, KT)
                use = None if m < 0 else (slab_used, (KT - 1) * b + kt + 1) if kt < KT - 1 \
                    else (bank_full, (4, 8, 10, PRO_BANKS)[b])
                split_hi(n % RING, (n // 2) % PAIRS, n // 2 // PAIRS + 1 if n % 2 == 0 else None, use)

            def split(g, s, hb=None):
                n = s + LEAD
                b, kt = divmod(n - RING, KT)
                more = (lambda x: 0) if hb is None else (lambda x: x * hb)
                if kt < KT - 1:
                    use = (slab_used, (KT - 1) * (PRO_SLABS // KT + GROUP_SLABS // KT * g + b) + kt + 1
                           + more(4 * (KT - 1)))
                else:
                    use = (bank_full, use_no(g, 4 * (b + 1) + (8 if b >= B_O else 0))
                           + more(16))
                fills = PRO_SLABS // 2 // PAIRS + GROUP_SLABS // 2 // PAIRS * g + n // 2 // PAIRS + 1 \
                    + more(2 * KT // PAIRS)
                split_hi(n % RING, (n // 2) % PAIRS, fills if n % 2 == 0 else None, use)

            def tile_hi(n, kt, width, gain):
                act.wait_ge(tr_full, n + 1)
                src = work[:, kt % 4, 0:width]
                if gain is None:
                    ins = nc.scalar.activation(act_hi[:, kt, 0:width], src, ACT.Copy)
                else:
                    ins = nc.scalar.activation(act_hi[:, kt, 0:width], src, ACT.Copy,
                                               scale=norm_g[:, gain, kt:kt + 1])
                ins.then_inc(act_hi_ready, 1)

            def sum_squares(i):
                nc.scalar.activation(tok[:, i, :], xres[:, i, :], ACT.Square,
                                     accum_out=ss[:, i:i + 1]).then_inc(norm_ss, 1)

            def guess(n, count):
                act.wait_ge(norm_var, count)
                mark(nc.scalar.activation(lnv[:, 0:n], var[:, 0:n], ACT.Ln))
                settle()
                nc.scalar.activation(y0[:, 0:n], lnv[:, 0:n], ACT.Exp, scale=-0.5).then_inc(norm_guess, 1)

            act.wait_ge(const_in, 16 * N_CONST)
            act.wait_ge(const_made, 1)
            nc.scalar.activation(wg_hi[:], wg_raw[:], ACT.Copy).then_inc(gate_w_hi, 1)
            for n in range(LEAD):
                split_pro(n)
            for i in range(2):
                sum_squares(i)
            guess(2, 1)
            for kt in range(KT):
                tile_hi(kt, kt, MEM, 3)
            for b in range(4):
                for s in range(KT):
                    split_pro(KT * b + s + LEAD)
                for i in range(4 if b < 2 else 2):
                    u = 4 * b + i if b < 2 else 8 + 2 * (b - 2) + i
                    act.wait_ge(bank_full, u + 1)
                    if b < 2:
                        ins = nc.scalar.activation(memK[:, 4 * b + i, :], bank[i][:, 0:MEM], ACT.Copy)
                    else:
                        ins = nc.scalar.activation(memV[:, i, (b - 2) * COLS:(b - 1) * COLS],
                                                   bank[2 * (b - 2) + i][:], ACT.Copy)
                    ins.then_inc(bank_free, 1)

            with act.Fori(0, NG) as g:
                start_group(g)

                def full(u):
                    act.wait_ge(bank_full, use_no(g, u + 1))

                def distance_exps(c):
                    act.wait_ge(z_abs, 4 * g + c + 1)
                    nc.scalar.activation(Z[:, c % 2], Z[:, c % 2], ACT.Exp, scale=-1.0 / TAU).then_inc(z_exp, 1)

                def sum_exps(c):
                    t0 = c * CH
                    if c == 0:
                        act.wait_ge(og_scaled, 8 * g + 8)
                    if c >= 2:
                        act.wait_ge(s_ready, 4 * g + c - 1)
                    nc.scalar.activation(eb[:, c % 2], decay[:, :, t0:t0 + CH], ACT.Exp, scale=1.0 / TAU)
                    act.wait_ge(bend_ready, 4 * g + c + 1)
                    for j in range(2):
                        ins = nc.scalar.activation(ekw[:, c % 2, j, :], decay[:, j, t0:t0 + CH], ACT.Exp,
                                                   scale=-1.0 / TAU, bias=bend[:, c % 2, j:j + 1])
                    ins.then_inc(ekw_ready, 1)

                def norm_tiles(k, gain, wait_x):
                    wait_x()
                    for i in range(NCH):
                        sum_squares(i)
                    guess(NCH, NORMS * g + k + 2)
                    t = {0: 0, 1: 16, 2: 24}.get(k)
                    if t is not None:
                        for kt in range(KT):
                            tile_hi(TRS * g + KT + t + kt, kt, GROUP, gain)

                nc.scalar.preload_act_table_set("natural_log_exp_and_others")

                def x_arrived():
                    act.wait_ge(x_in, 16 * NCH * (g + 1))
                norm_tiles(0, 0, x_arrived)
                for s in range(B_OUT * KT):
                    split(g, s)
                    b, r = divmod(s, KT)
                    if s == 2:
                        act.wait_ge(gates_full, g + 1)
                        src = work[:, 0, 0:NCH * 32].rearrange("p (c n) -> p c n", n=32)
                        nc.scalar.activation(gif[:].rearrange("p a c h -> p c a h"),
                                             src[:, :, 0:2 * HEADS].rearrange("p c (a h) -> p c a h", a=2), ACT.Copy)
                        nc.scalar.activation(gga[:], src[:, :, 2 * HEADS:NGATE], ACT.Copy).then_inc(gates_out, 1)
                    if s == 3:
                        act.wait_ge(grow_full, g + 1)
                        nc.scalar.activation(rows[:, R_LI:R_LF + 1, :],
                                                      work[0:16, 1, 0:2 * CH].rearrange("p (a t) -> p a t", a=2),
                                                      ACT.Copy)
                        nc.scalar.activation(gaT[:], work[0:RANK, 2, :], ACT.Copy).then_inc(grow_out, 1)
                    if s == 5:
                        act.wait_ge(grow_out, g + 1)
                        nc.scalar.activation(rtmp[:, 0, :], rows[:, R_LF, :], ACT.Abs, bias=gate_b[:, 1:2])
                        act.wait_ge(la_min, g + 1)
                        for j in range(2):
                            ins = nc.scalar.activation(decay[:, j, :], work[:, 3 * (1 - j), :], ACT.Abs,
                                                       bias=ba[:, j:j + 1])
                        ins.then_inc(la_abs, 1)
                    if b in (1, 2) and r % 2 == 1:
                        k = (b - 1) * 4 + r // 2
                        act.wait_ge(conv_done, KT * g + k + 1)
                        if k >= 2:
                            act.wait_ge(qk_ready, KT * g + k - 1)
                        nc.scalar.activation(sg[:, k % 2, :], qk[:, k, :], ACT.Sigmoid).then_inc(conv_sig, 1)
                    if r == KT - 1:
                        for i in range(4):
                            full(4 * b + i)
                            if b in (B_MQ, B_MK):
                                k = 4 * b + i
                                if b == B_MK:
                                    act.wait_ge(conv_done, KT * g + i + 1)
                                nc.scalar.activation(ubuf[:, i, 3:], bank[i][:], ACT.Copy)\
                                    .then_inc(bank_free, 1)
                            elif b == B_MO:
                                nc.scalar.activation(tok[:, i, 0:COLS], bank[i][:], ACT.Sigmoid)\
                                    .then_inc(bank_free, 1)
                            elif b == B_GR:
                                if i == 0:
                                    act.wait_ge(qk_ready, KT * g + KT)
                                if i >= 2:
                                    read_out(act, g, 4 * B_GR + i - 2)
                                nc.scalar.activation(sg[:, i % 2, :], bank[i][:], ACT.Sigmoid).then_inc(gr_sig, 1)
                            elif b == B_MV:
                                nc.scalar.activation(vext[:, i, :, 0:HD],
                                                     bank[i][:].rearrange("p (h n) -> p h n", h=HEADS),
                                                     ACT.Copy).then_inc(bank_free, 1)
                            elif b == B_GQK:
                                nc.scalar.activation(gqk[:, i, :], bank[i][:], ACT.Copy,
                                                     scale=DK ** -0.5 if i < 2 else 1.0)\
                                    .then_inc(bank_free, 1)
                            elif b == B_GV:
                                nc.scalar.activation(gv[:, i, :], bank[i][:], ACT.Copy)\
                                    .then_inc(bank_free, 1)
                    if s == 32:
                        nc.scalar.preload_act_table_set("natural_log_exp_and_others")
                        act.wait_ge(la_abs, g + 1)
                        mark(nc.scalar.activation(rtmp[:, 0, :], rtmp[:, 0, :], ACT.Exp, scale=-1.0))
                        mark(nc.scalar.activation(decay[:], decay[:], ACT.Exp, scale=-1.0))
                        settle()
                        nc.scalar.activation(rtmp[:, 0, :], rtmp[:, 0, :], ACT.Ln, bias=1.0).then_inc(row_log, 1)
                        nc.scalar.activation(decay[:], decay[:], ACT.Ln, bias=1.0).then_inc(la_log, 1)
                    if s == 35:
                        act.wait_ge(row_p, g + 1)
                        nc.scalar.activation(rows[:, R_WK, :], rows[:, R_A, :], ACT.Exp, bias=rcol[:, 1:2])
                        nc.scalar.activation(rows[:, R_EM, :], rows[:, R_EM, :], ACT.Exp, scale=-1.0)
                        nc.scalar.activation(rcol[:, 2:3], rcol[:, 0:1], ACT.Exp,
                                             bias=rcol[:, 1:2]).then_inc(row_exp, 1)
                    if s >= 40:
                        c, stage = divmod(s - 40, 4)
                        if stage == 0:
                            act.wait_ge(m_arg, 4 * g + c + 1)
                            nc.scalar.activation(arg, arg, ACT.Exp, scale=-1.0).then_inc(m_exp, 1)
                            for h in range(HEADS):
                                r16 = c * HEADS + h
                                ins = nc.scalar.activation(ew[:, h, :], work[:, 0, h * CH:(h + 1) * CH], ACT.Exp,
                                                           scale=-1.0, bias=bc[:, 1, r16:r16 + 1])
                            ins.then_inc(m_exp, 1)
                        if stage == 2:
                            act.wait_ge(num_out, 4 * g + c + 1)
                            for h in range(HEADS):
                                ins = nc.scalar.activation(
                                    ew[:, h, :], work[:, 2 + h // 2, 256 * (h % 2):256 * (h % 2) + HD], ACT.Square,
                                    accum_out=hss[:, 0, c, h:h + 1])
                            ins.then_inc(num_ss, 1)
                    if s in (50, 54):
                        distance_exps((s - 50) // 4)
                        sum_exps((s - 50) // 4)

                for c in range(NCH):
                    act.wait_ge(side_full, 4 * g + c + 1)
                    if c >= 1:
                        act.wait_ge(s_full, 4 * g + c)
                    nc.scalar.activation(kwT[:], work[:, 3, 256:512], ACT.Copy)
                    nc.scalar.activation(a2[:], work[0:64, 3, 0:256].rearrange("p (h t) -> p h t", h=HEADS),
                                         ACT.Copy).then_inc(side_out, 1)
                    if c + 2 < NCH:
                        distance_exps(c + 2)
                    act.wait_ge(o_out, 4 * g + c + 1)
                    for h in range(HEADS):
                        ins = nc.scalar.activation(qw[:, h, :], work[:, 2, h * HD:(h + 1) * HD], ACT.Square,
                                                   accum_out=hss[:, 1, c, h:h + 1])
                    ins.then_inc(o_ss, 1)
                    if c + 2 < NCH:
                        sum_exps(c + 2)

                act.wait_ge(h_var, g + 1)
                mark(nc.scalar.activation(hln[:], hvar[:], ACT.Ln))
                settle()
                nc.scalar.activation(hy0[:], hln[:], ACT.Exp, scale=-0.5).then_inc(h_guess, 1)
                for kt in range(KT):
                    tile_hi(TRS * g + KT + 8 + kt, kt, GROUP, None)
                for s in range(B_OUT * KT, B_Q * KT):
                    split(g, s)

                def mix_added():
                    read_out(act, g, U_OUT + 7)
                norm_tiles(1, 1, mix_added)
                for s in range(B_Q * KT, B_O * KT):
                    split(g, s)
                    if s % KT == KT - 1:
                        b = s // KT - B_Q
                        for i in range(4):
                            full(U_Q + 4 * b + i)
                            nc.scalar.activation(qk[:, 4 * b + i, :], bank[i][:], ACT.Copy,
                                                 scale=XHD ** -0.5).then_inc(bank_free, 1)
                for i in range(NCH):
                    act.wait_ge(sc_max, 4 * g + i + 1)
                    if i >= 2:
                        act.wait_ge(prT_full, 8 * g + 2 * (i - 1))
                    for h in range(HEADS):
                        ins = nc.scalar.activation(pr[:, i % 2, h, :],
                                                   work[:, 2 * (i % 2) + h // 2, 256 * (h % 2):256 * (h % 2) + MEM],
                                                   ACT.Exp, bias=smax[:, i % 2, h:h + 1],
                                                   accum_out=ssum[:, i % 2, h:h + 1])
                    ins.then_inc(sc_exp, 1)
                    for half in range(2):
                        act.wait_ge(prT_full, 8 * g + 2 * i + half + 1)
                        nc.scalar.activation(
                            prT[:, 2 * half:2 * half + 2, :, i * P:(i + 1) * P],
                            bank[2 * (i % 2) + half][:].rearrange("p (h m t) -> p h m t", h=2, m=2),
                            ACT.Copy).then_inc(prT_out, 1)
                for k in range(KT):
                    full(U_PV + k)
                    nc.scalar.activation(act_hi[:, k, :], bank[k % 4][:], ACT.Copy).then_inc(av_hi, 1)
                for s in range(B_O * KT, B_MLP * KT):
                    split(g, s)

                def attn_added():
                    read_out(act, g, U_O + 7)
                norm_tiles(2, 2, attn_added)
                with act.Fori(0, HB) as hb:
                    for s in range(4 * KT):
                        split(g, B_MLP * KT + s, hb)
                        b, r = divmod(s, KT)
                        if b < 2 and r == KT - 1:
                            for i in range(4):
                                k = 4 * b + i
                                n = 8 * HB * g + 8 * hb + k
                                act.wait_ge(bank_full, use_no(g, U_MLP + k + 1) + 16 * hb)
                                if b == 1:
                                    act.wait_ge(h_ready, n - 3)
                                nc.scalar.activation(hr[:, i, :], bank[i][:], ACT.Relu)\
                                    .then_inc(bank_free, 1)
                                read_out(act, g, U_MLP + k, 16 * hb)
                                nc.scalar.activation(h_hi[:, k, :], hr[:, i, :], ACT.Square).then_inc(sq_hi, 1)

                def mlp_added():
                    read_out(act, g, GROUP_BANKS - 1)
                norm_tiles(3, None, mlp_added)
                end_group()


        @block.vector
        def _(dve):
            mark, settle, start_group, end_group = own_results(dve, dve_step, DVE_BASE, DVE_PER)
            tt, ts, stt = nc.vector.tensor_tensor, nc.vector.tensor_scalar, nc.vector.scalar_tensor_tensor

            def link(ins):
                mark(ins)
                settle()

            def split_lo(n, slot, pair_slot):
                dve.wait_ge(slab_hi, n + 1)
                tt(w_lo[:, slot, :], raw[:, pair_slot, slot % 2, :], w_hi[:, slot, :].bitcast(F32),
                   ALU.subtract).then_inc(slab_lo, 1)

            def split_at(n):
                split_lo(n, n % RING, (n // 2) % PAIRS)

            def split(g, s, hb=None):
                n = s + LEAD
                base = slab_no(g, 0) if hb is None else slab_no(g, 0) + 4 * KT * hb
                split_lo(base + n, n % RING, (n // 2) % PAIRS)

            def tile_lo(count, kt, width, gain):
                dve.wait_ge(act_hi_ready, count + 1)
                src, hi, lo = work[:, kt % 4, 0:width], act_hi[:, kt, 0:width].bitcast(F32), act_lo[:, kt, 0:width]
                if gain is None:
                    tt(lo, src, hi, ALU.subtract).then_inc(act_lo_ready, 1)
                else:
                    stt(out=lo, in0=src, scalar=norm_g[:, gain, kt:kt + 1], in1=hi, op0=ALU.mult,
                        op1=ALU.subtract).then_inc(act_lo_ready, 1)

            def scale_rows(n, ss_count, k_count):
                dve.wait_ge(norm_ss, ss_count)
                ts(var[:, 0:n], ss[:, 0:n], 1.0 / D, EPS, ALU.mult, ALU.add).then_inc(norm_var, 1)
                dve.wait_ge(norm_guess, k_count)
                link(stt(out=y1[:, 0:n], in0=y0[:, 0:n], scalar=-0.5, in1=y0[:, 0:n], op0=ALU.mult, op1=ALU.mult))
                link(tt(y1[:, 0:n], y1[:, 0:n], var[:, 0:n], ALU.mult))
                link(stt(out=rstd[:, 0:n], in0=y1[:, 0:n], scalar=1.5, in1=y0[:, 0:n], op0=ALU.add, op1=ALU.mult))
                for i in range(n):
                    ts(tok[:, i, :], xres[:, i, :], rstd[:, i:i + 1], None, ALU.mult).then_inc(tok_ready, 1)

            dve.wait_ge(gate_w_hi, 1)
            tt(wg_lo[:], wg_raw[:], wg_hi[:].bitcast(F32), ALU.subtract).then_inc(gate_w_lo, 1)
            for n in range(LEAD):
                split_at(n)
            scale_rows(2, 2, 1)
            for kt in range(KT):
                tile_lo(kt, kt, MEM, 3)
            for n in range(LEAD, PRO_SLABS + LEAD):
                split_at(n)

            with dve.Fori(0, NG) as g:
                start_group(g)

                def full(u):
                    dve.wait_ge(bank_full, use_no(g, u + 1))

                def norm_tiles(k, gain):
                    scale_rows(NCH, 2 + 4 * NORMS * g + 4 * (k + 1), NORMS * g + k + 2)
                    t = {0: 0, 1: 16, 2: 24}.get(k)
                    if t is not None:
                        for kt in range(KT):
                            tile_lo(TRS * g + KT + t + kt, kt, GROUP, gain)

                def add_block(b, u, col):
                    for i in range(4):
                        full(u + i)
                        v = xres[:, i, col:col + COLS]
                        tt(v, bank[i][:], v, ALU.add).then_inc(bank_free, 1)

                def distance_abs(c):
                    t0 = c * CH
                    dve.wait_ge(z_diff, 4 * g + c + 1)
                    dve.wait_ge(gla_in, g + 1)
                    stt(out=Z[:, c % 2], in0=Z[:, c % 2], scalar=-1.0, in1=Z[:, c % 2], op0=ALU.mult,
                        op1=ALU.max).then_inc(z_abs, 1)
                    ts(bend[:, c % 2, :], decay[:, :, t0 + CH - 1], 1.0 / TAU, None, ALU.mult).then_inc(bend_ready, 1)

                def weigh_kq(c):
                    t0 = c * CH
                    if c == 0:
                        read_out(dve, g, 4 * B_GQK + 3)
                    dve.wait_ge(ekw_ready, 4 * g + c + 1)
                    if c >= 2:
                        dve.wait_ge(o_full, 4 * g + c - 1)
                    tt(ekw[:, c % 2], ekw[:, c % 2], gqk[:, 2:4, t0:t0 + CH], ALU.mult)
                    tt(qe[:, c % 2], eb[:, c % 2], gqk[:, 0:2, t0:t0 + CH], ALU.mult).then_inc(kq_ready, 1)

                def weigh_p(c):
                    tt(pdiag[:], rows[:, R_P, :].unsqueeze(1).to_broadcast([16, HEADS, CH]),
                       ident[0:16, c * HEADS:(c + 1) * HEADS].unsqueeze(2).to_broadcast([16, HEADS, CH]),
                       ALU.mult).then_inc(pdiag_ready, 1)

                norm_tiles(0, 0)
                nc.vector.memset(vext[:, :, :, HD:HD + 1], 1.0).then_inc(v_ones, 1)
                for s in range(B_OUT * KT):
                    split(g, s)
                    b, r = divmod(s, KT)
                    if s == 5:
                        dve.wait_ge(grow_out, g + 1)
                        ts(rtmp[:, 1, :], rows[:, R_LF, :], gate_b[:, 1:2], 0.0, ALU.add, ALU.min)
                        dve.wait_ge(la_full, g + 1)
                        for j in range(2):
                            z = work[:, 3 * (1 - j), :]
                            ins = ts(zmin[:, j, :], z, ba[:, j:j + 1], 0.0, ALU.add, ALU.min)
                        ins.then_inc(la_min, 1)
                    if b in (1, 2):
                        k, i = (b - 1) * 4 + r // 2, r // 2
                        if r % 2 == 0:
                            read_out(dve, g, k)
                            mark(nc.vector.tensor_copy(ubuf[:, i, 0:CONV - 1], halo[:, k, :]))
                            acc = qk[:, k, :]
                            settle()
                            link(ts(acc, ubuf[:, i, 0:GROUP], conv_w[:, 0, k:k + 1], conv_b[:, k:k + 1],
                                    ALU.mult, ALU.add))
                            for j in range(1, CONV):
                                ins = stt(out=acc, in0=ubuf[:, i, j:j + GROUP], scalar=conv_w[:, j, k:k + 1],
                                          in1=acc, op0=ALU.mult, op1=ALU.add)
                                if j < CONV - 1:
                                    link(ins)
                            nc.vector.tensor_copy(halo[:, k, :], ubuf[:, i, GROUP:]).then_inc(conv_done, 1)
                        else:
                            dve.wait_ge(conv_sig, KT * g + k + 1)
                            acc = qk[:, k, :]
                            tt(acc, acc, sg[:, k % 2, :], ALU.mult).then_inc(qk_ready, 1)
                    if b == B_GR and r == KT - 1:
                        for i in range(4):
                            dve.wait_ge(gr_sig, 4 * g + i + 1)
                            tt(tok[:, i, COLS:], bank[i][:], sg[:, i % 2, :], ALU.mult)\
                                .then_inc(bank_free, 1)
                    if s == 33:
                        dve.wait_ge(row_log, g + 1)
                        link(tt(rows[:, R_LF, :], rtmp[:, 1, :], rtmp[:, 0, :], ALU.subtract))
                        link(nc.vector.tensor_tensor_scan(rows[:, R_B, :], rows[:, R_LF, :], rows[:, R_LF, :], 0.0,
                                                          ALU.add, ALU.bypass))
                        link(stt(out=rows[:, R_A, :], in0=rows[:, R_LI, :], scalar=gate_b[:, 0:1],
                                 in1=rows[:, R_B, :], op0=ALU.add, op1=ALU.subtract))
                        nc.vector.tensor_tensor_scan(rows[:, R_M, :], rows[:, R_A, :], rows[:, R_A, :],
                                                     -3e38, ALU.max, ALU.bypass).then_inc(row_scan, 1)
                    if s == 34:
                        dve.wait_ge(mlast_full, g + 1)
                        link(nc.vector.tensor_copy(mlast[:], work[0:1, 1, 0:32].rearrange("p (a r) -> p a r", a=2)))
                        for h in range(HEADS):
                            ins = nc.vector.tensor_tensor_scan(
                                mrow[0:1, 1:NCH + 1, h], mlast[0:1, 0, h:16:HEADS], mlast[0:1, 1, h:16:HEADS],
                                mrow[0:1, 0, h:h + 1], ALU.max, ALU.add)
                        ins.then_inc(mrow_ready, 1)
                    if s == 35:
                        dve.wait_ge(mcol_full, g + 1)
                        link(nc.vector.tensor_copy(rcol[:, 0:1], work[0:16, 2, 0:1]))
                        link(ts(rows[:, R_P, :], rows[:, R_M, :], rcol[:, 0:1], None, ALU.max))
                        tt(rows[:, R_EM, :], rows[:, R_B, :], rows[:, R_P, :], ALU.add)
                        ts(rcol[:, 1:2], rows[:, R_P, CH - 1:CH], -1.0, None, ALU.mult).then_inc(row_p, 1)
                    if s == 36:
                        dve.wait_ge(row_exp, g + 1)
                        ts(diag[:, 0, :], ident[0:16, 0:16], rcol[:, 2:3], None, ALU.mult)
                        ts(diag[:, 1, :], ident[0:16, 0:16], rcol[:, 0:1], None, ALU.mult).then_inc(diag_ready, 1)
                        nc.vector.tensor_copy(mrow[0:1, 0, :], mrow[0:1, NCH, :])
                        weigh_p(0)
                    if s == 37:
                        dve.wait_ge(cols_full, g + 1)
                        nc.vector.tensor_copy(bc[:], work[:, 1, 0:32].rearrange("p (a r) -> p a r", a=2))
                        nc.vector.tensor_copy(cols[:], work[:, 2, 0:48].rearrange("p (a r) -> p a r", a=3))\
                            .then_inc(cols_ready, 1)
                    if s == 38:
                        dve.wait_ge(la_log, g + 1)
                        link(tt(decay[:], zmin[:], decay[:], ALU.subtract))
                        for j in range(2):
                            for c in range(NCH):
                                v = decay[:, j, c * CH:(c + 1) * CH]
                                ins = nc.vector.tensor_tensor_scan(v, v, v, 0.0, ALU.add, ALU.bypass)
                        ins.then_inc(gla_in, 1)
                    if s >= 40:
                        c, stage = divmod(s - 40, 4)
                        t0 = c * CH
                        if stage == 0:
                            dve.wait_ge(ps_full, 4 * g + c + 1)
                            dve.wait_ge(cols_ready, g + 1)
                            for h in range(HEADS):
                                ins = stt(out=arg[:, h, :], in0=work[:, 0, h * CH:(h + 1) * CH],
                                          scalar=cols[:, 0, c * HEADS + h:c * HEADS + h + 1], in1=causal[:],
                                          op0=ALU.subtract, op1=ALU.add)
                            ins.then_inc(m_arg, 1)
                            dve.wait_ge(m_exp, 8 * g + 2 * c + 1)
                            stt(out=sm, in0=work[:, 1, :].rearrange("p (h t) -> p h t", h=HEADS),
                                scalar=HD ** -0.5, in1=arg, op0=ALU.mult, op1=ALU.mult)
                            dve.wait_ge(m_exp, 8 * g + 2 * c + 2)
                            stt(out=qw, in0=qk[:, 0:HEADS, t0:t0 + CH], scalar=HD ** -0.5, in1=ew,
                                op0=ALU.mult, op1=ALU.mult).then_inc(m_in, 1)
                        if stage == 1:
                            dve.wait_ge(kt_full, 4 * g + c + 1)
                            tt(wk[:], work[:, 0, :].rearrange("p (h d) -> p h d", h=HEADS),
                               cols[:, 1, c * HEADS:(c + 1) * HEADS].unsqueeze(2).to_broadcast([P, HEADS, HD]),
                               ALU.mult).then_inc(wk_ready, 1)
                            if c + 1 < NCH:
                                weigh_p(c + 1)
                        if stage == 2:
                            dve.wait_ge(num_full, 4 * g + c + 1)
                            dve.wait_ge(og_scaled, 8 * g + 4)
                            num = work[:, 2:4, :].rearrange("p b (h n) -> p (b h) n", h=2)
                            v = tok[:, c, 0:COLS].rearrange("p (h n) -> p h n", h=HEADS)
                            tt(v, num[:, :, 0:HD], v, ALU.mult)
                            nc.vector.tensor_copy(hden[:, c, :], num[:, :, HD]).then_inc(num_out, 1)
                        if stage == 3:
                            dve.wait_ge(c_full, 4 * g + c + 1)
                            upd = work[:, 0:2, :].rearrange("p b (h n) -> p (b h) n", h=2)
                            if c >= 1:
                                dve.wait_ge(c_ready, 4 * g + c)
                            for h in range(HEADS):
                                ins = stt(out=stC[:, h, :], in0=stC[:, h, :],
                                          scalar=bc[:, 0, c * HEADS + h:c * HEADS + h + 1],
                                          in1=upd[:, h, 0:HD + 1], op0=ALU.mult, op1=ALU.add)
                            ins.then_inc(c_ready, 1)
                    if s == 50:
                        distance_abs(0)
                        weigh_kq(0)
                    if s == 54:
                        distance_abs(1)
                        weigh_kq(1)

                for c in range(NCH):
                    for hd in range(HEADS):
                        n = 16 * g + 4 * c + hd + 1
                        dve.wait_ge(lvl_full, n)
                        pl = work[:, hd % 2, 0:7 * 64].rearrange("p (l t) -> p l t", l=7)
                        tt(msk[:, hd % 2], pl, lvl_mask[:], ALU.mult).then_inc(lvl_masked, 1)
                        dve.wait_ge(lvl_masked, n)
                        if hd == 0 and c >= 1:
                            dve.wait_ge(o_full, 4 * g + c)
                        nc.vector.tensor_reduce(ad[:, hd, :], msk[:, hd % 2].rearrange("p l t -> p t l"), AX.X,
                                                ALU.add).then_inc(ad_ready, 1)
                    if c + 2 < NCH:
                        distance_abs(c + 2)
                    dve.wait_ge(o_full, 4 * g + c + 1)
                    dve.wait_ge(og_scaled, 8 * g + 8)
                    v = tok[:, c, COLS:]
                    tt(v, work[:, 2, :], v, ALU.mult).then_inc(o_out, 1)
                    dve.wait_ge(s_full, 4 * g + c + 1)
                    if c >= 1:
                        dve.wait_ge(s_ready, 4 * g + c)
                    for j in range(2):
                        ins = stt(out=stS[:, j, :], in0=stS[:, j, :], scalar=eb[:, c % 2, j, CH - 1:CH],
                                  in1=work[:, 3, j * HD:(j + 1) * HD], op0=ALU.mult, op1=ALU.add)
                    ins.then_inc(s_ready, 1)
                    if c + 2 < NCH:
                        weigh_kq(c + 2)

                dve.wait_ge(num_ss, 4 * g + 4)
                dve.wait_ge(num_out, 4 * g + 4)
                fl = [x.rearrange("p c h -> p (c h)") for x in (hden[:], hinv[:], hvar[:, 0], hss[:, 0])]
                link(stt(out=fl[0], in0=fl[0], scalar=-1.0, in1=fl[0], op0=ALU.mult, op1=ALU.max))
                link(tt(fl[0], fl[0], cols[:, 2, :], ALU.max))
                link(nc.vector.reciprocal(fl[1], fl[0]))
                link(tt(fl[2], fl[1], fl[1], ALU.mult))
                link(tt(fl[2], fl[2], fl[3], ALU.mult))
                dve.wait_ge(o_ss, 4 * g + 4)
                link(ts(hvar[:, 0], hvar[:, 0], 1.0 / HD, EPS, ALU.mult, ALU.add))
                ts(hvar[:, 1], hss[:, 1], 1.0 / HD, EPS, ALU.mult, ALU.add).then_inc(h_var, 1)
                dve.wait_ge(h_guess, g + 1)
                link(stt(out=hy1[:], in0=hy0[:], scalar=-0.5, in1=hy0[:], op0=ALU.mult, op1=ALU.mult))
                link(tt(hy1[:], hy1[:], hvar[:], ALU.mult))
                link(stt(out=hscale[:], in0=hy1[:], scalar=1.5, in1=hy0[:], op0=ALU.add, op1=ALU.mult))
                link(tt(hscale[:, 0], hscale[:, 0], hinv[:], ALU.mult))
                for half in range(2):
                    v = tok[:, :, half * COLS:(half + 1) * COLS].rearrange("p c (h n) -> p c h n", h=HEADS)
                    tt(v, v, hscale[:, half].unsqueeze(3).to_broadcast([P, NCH, HEADS, HD]),
                       ALU.mult).then_inc(mixed, 1)
                for kt in range(KT):
                    tile_lo(TRS * g + KT + 8 + kt, kt, GROUP, None)
                for s in range(B_OUT * KT, B_Q * KT):
                    split(g, s)
                    if s % KT == KT - 1:
                        b = s // KT - B_OUT
                        add_block(b, U_OUT + 4 * b, b * COLS)
                norm_tiles(1, 1)

                for s in range(B_Q * KT, B_O * KT):
                    split(g, s)
                for i in range(NCH):
                    e = i % 2
                    sc = work[:, 2 * e:2 * e + 2, :].rearrange("p b (h m) -> p (b h) m", h=2)
                    dve.wait_ge(sc_full, 4 * g + i + 1)
                    link(nc.vector.tensor_reduce(smax[:, e, :], sc, AX.X, ALU.max))
                    ts(smax[:, e, :], smax[:, e, :], -1.0, None, ALU.mult).then_inc(sc_max, 1)
                    dve.wait_ge(sc_exp, 4 * g + i + 1)
                    link(nc.vector.reciprocal(sinv[:, e, :], ssum[:, e, :]))
                    tt(pr[:, e], pr[:, e], sinv[:, e, :].unsqueeze(2).to_broadcast([P, HEADS, MEM]),
                       ALU.mult).then_inc(pr_ready, 1)
                for k in range(KT):
                    dve.wait_ge(av_hi, KT * g + k + 1)
                    tt(act_lo[:, k, :], bank[k % 4][:], act_hi[:, k, :].bitcast(F32),
                       ALU.subtract).then_inc(bank_free, 1)
                for s in range(B_O * KT, B_MLP * KT):
                    split(g, s)
                    if s % KT == KT - 1:
                        b = s // KT - B_O
                        add_block(b, U_O + 4 * b, b * COLS)
                norm_tiles(2, 2)

                with dve.Fori(0, HB) as hb:
                    for s in range(4 * KT):
                        split(g, B_MLP * KT + s, hb)
                        b, r = divmod(s, KT)
                        if r == KT - 1 and b < 2:
                            for i in range(4):
                                k = 4 * b + i
                                n = 8 * HB * g + 8 * hb + k
                                read_out(dve, g, U_MLP + k, 16 * hb)
                                tt(hsq[:, i % 2, :], hr[:, i, :], hr[:, i, :], ALU.mult).then_inc(h_sq, 1)
                                dve.wait_ge(h_sq, n + 1)
                                dve.wait_ge(sq_hi, n + 1)
                                tt(h_lo[:, k, :], hsq[:, i % 2, :], h_hi[:, k, :].bitcast(F32),
                                   ALU.subtract).then_inc(h_ready, 1)
                        if r == KT - 1 and b >= 2:
                            for i in range(4):
                                dve.wait_ge(bank_full, use_no(g, U_MLP + 4 * b + i + 1) + 16 * hb)
                                v = xres[:, i, (b - 2) * COLS:(b - 1) * COLS]
                                tt(v, bank[i][:], v, ALU.add).then_inc(bank_free, 1)
                scale_rows(NCH, 2 + 4 * NORMS * g + 16, NORMS * g + 5)
                end_group()

        @block.tensor
        def _(pe):
            mm, transpose = nc.tensor.matmul, nc.tensor.transpose
            mark, settle, start_group, end_group = own_results(pe, pe_step, 0, PE_PER)

            def slab(n, kt, major, prior, a_hi, a_lo, width=GROUP, tiles=4, bank0=0):
                slot = kt % RING
                pe.wait_ge(slab_lo, n + 1)
                for i in range(tiles):
                    if kt == 0 and prior is not None:
                        pe.wait_ge(bank_free, prior + i + 1)
                    dst = bank[bank0 + i][:, 0:width]
                    here = slice(i * P, (i + 1) * P)
                    if major == "feature":
                        terms = ((w_hi[:, slot, here], a_hi[:, kt, 0:width]),
                                 (w_hi[:, slot, here], a_lo[:, kt, 0:width]),
                                 (w_lo[:, slot, here], a_hi[:, kt, 0:width]))
                    else:
                        terms = ((a_hi[:, kt, here], w_hi[:, slot, :]),
                                 (a_hi[:, kt, here], w_lo[:, slot, :]),
                                 (a_lo[:, kt, here], w_hi[:, slot, :]))
                    for j, (left, right) in enumerate(terms):
                        ins = mm(dst, left, right, start=(kt == 0 and j == 0), stop=(kt == KT - 1 and j == 2))
                    if kt == KT - 1:
                        ins.then_inc(bank_full, 1)
                if kt < KT - 1:
                    ins.then_inc(slab_used, 1)

            def tiles_out(count0, ready, src_rows):
                for kt in range(KT):
                    if kt in ready:
                        pe.wait_ge(*ready[kt])
                    if kt >= 4:
                        pe.wait_ge(act_lo_ready, count0 + kt - 3)
                    for i in range(src_rows):
                        ins = transpose(work[:, kt % 4, i * P:(i + 1) * P], tok[:, i, kt * P:(kt + 1) * P], ident[:])
                    ins.then_inc(tr_full, 1)

            pe.wait_ge(const_made, 1)
            tiles_out(0, {0: (tok_ready, 2)}, 2)
            for b in range(4):
                for kt in range(KT):
                    if b == 0:
                        pe.wait_ge(act_lo_ready, kt + 1)
                    if b < 2:
                        slab(KT * b + kt, kt, "feature", None if b == 0 else 0, act_hi, act_lo, MEM)
                    else:
                        slab(KT * b + kt, kt, "token", 4 + 2 * (b - 2), act_hi, act_lo, COLS, 2, 2 * (b - 2))
            pe.wait_ge(gate_w_lo, 1)

            with pe.Fori(0, NG) as g:
                start_group(g)

                def block_slab(s, major, u, tile_count=None, a_hi=act_hi, a_lo=act_lo):
                    kt = s % KT
                    if tile_count is not None:
                        pe.wait_ge(act_lo_ready, TRS * g + KT + tile_count + kt + 1)
                    slab(slab_no(g, s), kt, major, use_no(g, u - 4), a_hi, a_lo)

                tiles_out(TRS * g + KT, {0: (tok_ready, 16 * g + 2 + 4)}, NCH)
                for s in range(B_OUT * KT):
                    b = s // KT
                    if s == 2:
                        pe.wait_ge(act_lo_ready, TRS * g + 2 * KT)
                        for i in range(NCH):
                            for kt in range(KT):
                                here = slice(i * P, (i + 1) * P)
                                for j, (left, right) in enumerate(((act_hi, wg_hi), (act_hi, wg_lo), (act_lo, wg_hi))):
                                    ins = mm(work[:, 0, 32 * i:32 * i + NGATE], left[:, kt, here], right[:, kt, :],
                                             start=(kt == 0 and j == 0), stop=(kt == KT - 1 and j == 2))
                        ins.then_inc(gates_full, 1)
                    if s == 3:
                        pe.wait_ge(gates_out, g + 1)
                        for k in range(2):
                            transpose(work[0:16, 1, k * CH:(k + 1) * CH], gif[:, k].rearrange("p c h -> p (c h)"), ident[:])
                        for i in range(NCH):
                            ins = transpose(work[0:RANK, 2, i * P:(i + 1) * P], gga[:, i, :], ident[:])
                        ins.then_inc(grow_full, 1)
                    if s == 5:
                        pe.wait_ge(grow_out, g + 1)
                        for j in range(2):
                            ins = mm(work[:, 3 * (1 - j), :], wa2[:, j * P:(j + 1) * P], gaT[:], start=True, stop=True)
                        ins.then_inc(la_full, 1)
                    if s == 34:
                        pe.wait_ge(row_scan, g + 1)
                        stand_alone(pe)
                        for k, row in enumerate((R_M, R_B)):
                            ins = transpose(work[0:1, 1, 16 * k:16 * k + 16], rows[:, row, CH - 1:CH], ident[0:16, 0:16])
                        ins.then_inc(mlast_full, 1)
                    if s == 35:
                        pe.wait_ge(mrow_ready, g + 1)
                        stand_alone(pe)
                        mm(work[0:16, 2, 0:1], mrow[0:1, 0:NCH, :].rearrange("p c h -> p (c h)"), ones16[0:1, 0:1],
                           start=True, stop=True).then_inc(mcol_full, 1)
                    if s == 37:
                        pe.wait_ge(diag_ready, g + 1)
                        mm(work[:, 1, 0:32], ones16[:], diag[:].rearrange("p a r -> p (a r)"), start=True, stop=True)
                        for k, row in enumerate((R_A, R_WK, R_EM)):
                            ins = transpose(work[:, 2, 16 * k:16 * k + 16], rows[:, row, :], ident[0:16, 0:16])
                        ins.then_inc(cols_full, 1)
                    if s >= 40:
                        c, stage = divmod(s - 40, 4)
                        t0 = c * CH
                        if stage == 0:
                            pe.wait_ge(pdiag_ready, 4 * g + c + 1)
                            pe.wait_ge(qk_ready, KT * g + KT)
                            if c == 0:
                                pe.wait_ge(cols_ready, g + 1)
                                pe.wait_ge(la_abs, g + 1)
                                pe.wait_ge(la_min, g + 1)
                            else:
                                pe.wait_ge(c_ready, 4 * g + c)
                            mm(work[:, 0, :], ones16[:], pdiag[:].rearrange("p h t -> p (h t)"), start=True, stop=True)
                            for h in range(HEADS):
                                ins = mm(work[:, 1, h * CH:(h + 1) * CH], qk[:, HEADS + h, t0:t0 + CH],
                                         qk[:, h, t0:t0 + CH], start=True, stop=True)
                            ins.then_inc(ps_full, 1)
                        if stage == 1:
                            pe.wait_ge(m_in, 4 * g + c + 1)
                            for h in range(HEADS):
                                ins = transpose(work[:, 0, h * HD:(h + 1) * HD], qk[:, HEADS + h, t0:t0 + CH], ident[:])
                            ins.then_inc(kt_full, 1)
                        if stage == 2:
                            read_out(pe, g, 4 * B_MV + 3)
                            pe.wait_ge(v_ones, g + 1)
                            if c >= 1:
                                pe.wait_ge(c_ready, 4 * g + c)
                                pe.wait_ge(num_out, 4 * g + c)
                                pe.wait_ge(num_ss, 4 * g + c)
                            for h in range(HEADS):
                                dst = work[:, 2 + h // 2, 256 * (h % 2):256 * (h % 2) + HD + 1]
                                mm(dst, qw[:, h, :], stC[:, h, :], start=True, stop=False)
                                ins = mm(dst, sm[:, h, :], vext[:, c, h, :], start=False, stop=True)
                            ins.then_inc(num_full, 1)
                        if stage == 3:
                            pe.wait_ge(wk_ready, 4 * g + c + 1)
                            for h in range(HEADS):
                                ins = mm(work[:, h // 2, 256 * (h % 2):256 * (h % 2) + HD + 1], wk[:, h, :],
                                         vext[:, c, h, :], start=True, stop=True)
                            ins.then_inc(c_full, 1)
                    block_slab(s, "feature" if b in (B_MQ, B_MK, B_GQK) else "token", 4 * b, 0 if b == B_MQ else None)

                def other_rows(ins):
                    mark(ins)
                    settle()
                    stand_alone(pe)

                def levels(c, hds):
                    pe.wait_ge(z_ready, 4 * g + c + 1)
                    t0 = c * CH
                    for hd in hds:
                        j, p0 = hd // 2, 64 * (hd % 2)
                        if 4 * c + hd >= 2:
                            pe.wait_ge(lvl_masked, 16 * g + 4 * c + hd - 1)
                        stand_alone(pe)
                        for q0 in (0, 64):
                            for lv in range(7):
                                dst = work[q0:q0 + 64, hd % 2, 64 * lv:64 * lv + 64]
                                if lv < 6:
                                    z = Z[p0:p0 + 64, c % 2, lv + 1, j * CH + q0:j * CH + q0 + 64]
                                    ins = mm(dst, z, z, start=True, stop=True)
                                else:
                                    here = slice(t0 + q0, t0 + q0 + 64)
                                    ins = mm(dst, gqk[p0:p0 + 64, 2 + j, here], gqk[p0:p0 + 64, j, here],
                                             start=True, stop=True)
                        ins.then_inc(lvl_full, 1)

                def side(c):
                    pe.wait_ge(kq_ready, 4 * g + c + 1)
                    if c >= 1:
                        pe.wait_ge(s_ready, 4 * g + c)
                    stand_alone(pe)
                    for hd in (0, 2, 1, 3):
                        j, p0 = hd // 2, 64 * (hd % 2)
                        ins = mm(work[0:64, 3, 64 * hd:64 * hd + 64], Z[p0:p0 + 64, c % 2, 0, j * CH:j * CH + 64],
                                 Z[p0:p0 + 64, c % 2, 0, j * CH + 64:j * CH + 128], start=True, stop=True)
                        if hd == 2:
                            other_rows(ins)
                    for j in range(2):
                        ins = transpose(work[:, 3, 256 + j * P:256 + (j + 1) * P], ekw[:, c % 2, j, :], ident[:])
                    ins.then_inc(side_full, 1)

                pe.wait_ge(c_ready, 4 * g + 4)
                pe.wait_ge(num_out, 4 * g + 4)
                pe.wait_ge(num_ss, 4 * g + 4)
                read_out(pe, g, 4 * B_GV + 3)
                levels(0, (0, 1))
                side(0)
                levels(0, (2, 3))
                for c in range(NCH):
                    if c + 1 < NCH:
                        levels(c + 1, (0, 1))
                    pe.wait_ge(ad_ready, 16 * g + 4 * c + 4)
                    pe.wait_ge(side_out, 4 * g + c + 1)
                    if c >= 1:
                        pe.wait_ge(o_out, 4 * g + c)
                        pe.wait_ge(o_ss, 4 * g + c)
                    cut = [slice(hd * HD, (hd + 1) * HD) for hd in range(HEADS)]
                    for hd in (0, 2, 1, 3):
                        j, p0 = hd // 2, 64 * (hd % 2)
                        ins = mm(work[:, 2, cut[hd]], qe[p0:p0 + 64, c % 2, j, :], stS[p0:p0 + 64, j, :],
                                 start=(hd == 0), stop=False, skip_group_check=True)
                        if hd == 2:
                            other_rows(ins)
                    for hd in range(HEADS):
                        mm(work[0:64, 2, cut[hd]], ad[0:64, hd, :], gv[0:64, c, cut[hd]], start=False, stop=True,
                           skip_group_check=True)
                        ins = mm(work[64:128, 2, cut[hd]], ad[64:128, hd, :], gv[64:128, c, cut[hd]],
                                 start=False, stop=False, skip_group_check=True)
                    other_rows(ins)
                    for hd in range(HEADS):
                        ins = mm(work[64:128, 2, cut[hd]], a2[:, hd, :], gv[0:64, c, cut[hd]], start=False, stop=True,
                                 skip_group_check=True)
                    ins.then_inc(o_full, 1)
                    for hd in range(HEADS):
                        j, p0 = hd // 2, 64 * (hd % 2)
                        ins = mm(work[p0:p0 + 64, 3, j * HD:(j + 1) * HD], kwT[:, hd * DK:(hd + 1) * DK],
                                 gv[:, c, hd * HD:(hd + 1) * HD], start=True, stop=True)
                    ins.then_inc(s_full, 1)
                    if c + 1 < NCH:
                        side(c + 1)
                        levels(c + 1, (2, 3))

                tiles_out(TRS * g + KT + 8, {0: (mixed, 2 * g + 1), 4: (mixed, 2 * g + 2)}, NCH)
                for s in range(B_OUT * KT, B_Q * KT):
                    b = s // KT - B_OUT
                    block_slab(s, "token", U_OUT + 4 * b, 8 if b == 0 else None)

                tiles_out(TRS * g + KT + 16, {0: (tok_ready, 16 * g + 2 + 8)}, NCH)
                for s in range(B_Q * KT, B_O * KT):
                    b = s // KT - B_Q
                    block_slab(s, "feature", U_Q + 4 * b, 16 if b == 0 else None)

                def scores(i):
                    if i >= 2:
                        pe.wait_ge(sc_exp, 4 * g + i - 1)
                    for h in range(HEADS):
                        for k in range(2):
                            ins = mm(work[:, 2 * (i % 2) + h // 2, 256 * (h % 2):256 * (h % 2) + MEM],
                                     qk[:, 2 * h + k, i * P:(i + 1) * P], memK[:, 2 * h + k, :],
                                     start=(k == 0), stop=(k == 1))
                    ins.then_inc(sc_full, 1)

                def turn_probs(i):
                    pe.wait_ge(pr_ready, 4 * g + i + 1)
                    for half in range(2):
                        if i >= 2:
                            pe.wait_ge(prT_out, 8 * g + 2 * (i - 2) + half + 1)
                        for k in range(4):
                            ins = transpose(bank[2 * (i % 2) + half][:, k * P:(k + 1) * P],
                                            pr[:, i % 2, 2 * half + k // 2, (k % 2) * P:(k % 2 + 1) * P], ident[:])
                        ins.then_inc(prT_full, 1)

                read_out(pe, g, U_Q + 7)
                scores(0)
                scores(1)
                for i in range(NCH):
                    turn_probs(i)
                    if i + 2 < NCH:
                        scores(i + 2)
                pe.wait_ge(prT_out, 8 * g + 8)
                for k in range(KT):
                    pe.wait_ge(bank_free, use_no(g, U_PV + k - 4) + 1)
                    for m in range(2):
                        ins = mm(bank[k % 4][:], memV[:, m, k * P:(k + 1) * P], prT[:, k // 2, m, :],
                                 start=(m == 0), stop=(m == 1))
                    ins.then_inc(bank_full, 1)
                for s in range(B_O * KT, B_MLP * KT):
                    b = s // KT - B_O
                    if b == 0:
                        read_out(pe, g, U_PV + s % KT)
                    block_slab(s, "token", U_O + 4 * b)

                tiles_out(TRS * g + KT + 24, {0: (tok_ready, 16 * g + 2 + 12)}, NCH)
                pe.wait_ge(act_lo_ready, TRS * g + KT + 32)
                stand_alone(pe)
                with pe.Fori(0, HB) as hb:
                    for s in range(4 * KT):
                        b, kt = divmod(s, KT)
                        if b == 2:
                            pe.wait_ge(h_ready, 8 * HB * g + 8 * hb + kt + 1)
                        slab(slab_no(g, B_MLP * KT + s) + 4 * KT * hb, kt, "feature" if b < 2 else "token",
                             use_no(g, U_MLP + 4 * b - 4) + 16 * hb,
                             act_hi if b < 2 else h_hi, act_lo if b < 2 else h_lo)
                end_group()


N_CONST = 12 + 2 * NCH
ACT_BASE, ACT_PER = 1, 7
DVE_BASE, DVE_PER = 3, 69
PE_PER = 3 * NCH
POOL_BASE, POOL_PER = 47, 4

_INS = ['x', 'mem', 'mix_norm_g', 'w_in', 'conv_w', 'conv_b', 'mlstm_i_b', 'mlstm_f_b', 'mlstm_norm_g',
        'gla_wa2', 'gla_ba', 'gla_norm_g', 'w_out', 'xattn_norm_g', 'mem_norm_g', 'wq_x', 'wk_x', 'wv_x',
        'wo_x', 'mlp_norm_g', 'w1', 'w2', 'final_norm_g']


_BY_FEATURE = ('mix_norm_g', 'xattn_norm_g', 'mlp_norm_g', 'mem_norm_g', 'conv_w', 'conv_b', 'gla_ba')


def kernel(**inputs):
    import numpy as _np
    import concourse.bacc as _bacc
    from concourse import mybir as _mybir
    from concourse.bass_utils import run_bass_kernel_spmd as _run

    nc = _bacc.Bacc("TRN2", target_bir_lowering=False, num_devices=1)
    arrays, args = {}, {}
    for name in _INS:
        a = _np.ascontiguousarray(inputs[name])
        if name != 'final_norm_g':
            a = a.reshape(a.shape[1:])
        if name in _BY_FEATURE:
            a = _np.ascontiguousarray(_np.moveaxis(a.reshape(*a.shape[:-1], -1, 128), -1, 0))
        arrays[f"in_{name}_dram"] = a
        args[name] = nc.dram_tensor(f"in_{name}_dram", a.shape, _mybir.dt.from_np(a.dtype), kind="ExternalInput").ap()
    out = nc.dram_tensor("out_dram", (SEQ, D), _mybir.dt.float32, kind="ExternalOutput").ap()
    program(nc, args, out)
    r = _run(nc, [arrays], core_ids=[0])
    return r.results[0]["out_dram"].reshape(1, SEQ, D)
```

```python
from contextlib import ExitStack

import numpy as np

import concourse.bass as bass
from concourse import mybir

F32 = mybir.dt.float32
F32R = mybir.dt.float32r
ACT = mybir.ActivationFunctionType
ALU = mybir.AluOpType
AX = mybir.AxisListType

P = 128
D = 1024
SEQ = 2048
GROUP = 512
CH = 128
NCH = GROUP // CH
NG = SEQ // GROUP
MEM = 256
KT = D // P
COLS = 512
HEADS = 4
HD = 128
DK = 64
XHD = 256
FF = 4096
CONV = 4
RANK = 16
EPS = 1e-6
BIG = 1e30
TAU = 16.0

C_MQ, C_MK, C_MV, C_MO = 0, 512, 1024, 1536
C_MI = 2048
C_GQ = 2056
C_GV = 2568
C_GR = 3080
C_GA = 3592
NGATE = 2 * HEADS + RANK

RING = 4
LEAD = 3
PAIRS = 4

B_MQ, B_MK, B_MO, B_GR, B_MV, B_GQK, B_GV, B_OUT, B_Q, B_O, B_MLP = 0, 1, 2, 3, 4, 5, 6, 7, 9, 11, 13
HB = FF // D
GROUP_SLABS = (B_MLP + 4 * HB) * KT
PRO_SLABS = 4 * KT
GROUP_BANKS = 4 * (B_MLP + 4 * HB + 2)
PRO_BANKS = 12
U_OUT, U_Q, U_PV, U_O, U_MLP = 28, 36, 44, 52, 60

TRS = 32
PRO_TR = 2 * KT
LEVELS = 7
M_SLAB = 38
G_SLAB = 55
EARLY = (KT + 2, KT + 3, KT + 4, KT + 5)
NORMS = 4
PRO_NORMS = 2
PRO_ROWS = MEM // P + NCH


def program(nc, A, out):
    ctx = ExitStack()
    with ctx:
        def sb(name, shape, dt=F32, stack=None):
            return (stack or ctx).enter_context(nc.sbuf_tensor(name, shape, dt))

        def sem(name):
            return ctx.enter_context(nc.semaphore(name))

        ident = sb("ident", [P, P])
        ones16 = sb("ones16", [16, P])
        causal = sb("causal", [P, P])
        lvl_mask = sb("lvl_mask", [P, 7, 64])
        norm_g = sb("norm_g", [P, 4, KT])
        conv_w = sb("conv_w", [P, CONV, KT])
        conv_b = sb("conv_b", [P, KT])
        gate_b = sb("gate_b", [16, 2])
        wa2 = sb("wa2", [RANK, 256])
        ba = sb("ba", [P, 2])
        sel = sb("sel", [NGATE, 2, 28])
        wg_raw = sb("wg_raw", [P, KT, NGATE])
        wg_hi = sb("wg_hi", [P, KT, NGATE], F32R)
        wg_lo = sb("wg_lo", [P, KT, NGATE], F32R)

        xres = sb("xres", [P, NCH, D])
        tok = sb("tok", [P, NCH, D])
        act_hi = sb("act_hi", [P, KT, GROUP], F32R)
        act_lo = sb("act_lo", [P, KT, GROUP], F32R)
        raw = sb("raw", [P, PAIRS, 2, COLS])
        w_hi = sb("w_hi", [P, RING, COLS], F32R)
        w_lo = sb("w_lo", [P, RING, COLS], F32R)
        memK = sb("memK", [P, KT, MEM])
        memV = sb("memV", [P, 2, D])
        qk = sb("qk", [P, KT, GROUP])
        halo = sb("halo", [P, KT, CONV - 1])
        stC = sb("stC", [P, HEADS, HD + 1])
        stS = sb("stS", [P, 2, HD])
        mrow = sb("mrow", [1, NCH + 1, HEADS])
        ss = sb("ss", [P, NCH])
        var = sb("var", [P, NCH])
        lnv = sb("lnv", [P, NCH])
        y0 = sb("y0", [P, NCH])
        y1 = sb("y1", [P, NCH])
        rstd = sb("rstd", [P, NCH])
        rs_attn = sb("rs_attn", [P, NCH])
        rs_mlp = sb("rs_mlp", [P, NCH])
        hss = sb("hss", [P, 2, NCH, HEADS])
        hinv = sb("hinv", [P, NCH, HEADS])
        hden = sb("hden", [P, NCH, HEADS])
        hvar = sb("hvar", [P, 2, NCH, HEADS])
        hln = sb("hln", [P, 2, NCH, HEADS])
        hy0 = sb("hy0", [P, 2, NCH, HEADS])
        hy1 = sb("hy1", [P, 2, NCH, HEADS])
        hscale = sb("hscale", [P, 2, NCH, HEADS])

        mixing = ExitStack()
        vext = sb("vext", [P, NCH, HEADS, HD + 1], F32, mixing)
        gqk = sb("gqk", [P, 4, GROUP], F32, mixing)
        gv = sb("gv", [P, NCH, COLS], F32, mixing)
        decay = sb("decay", [P, 2, GROUP], F32, mixing)
        zz = sb("zz", [P, 2 * LEVELS * 256], F32, mixing)
        Z = zz[:, :].rearrange("p (b l n) -> p b l n", b=2, l=LEVELS)
        ubuf = zz[:, 0:4 * (GROUP + 3)].rearrange("p (i n) -> p i n", i=4)
        zmin = zz[:, 4 * (GROUP + 3):4 * (GROUP + 3) + 2 * GROUP].rearrange("p (j n) -> p j n", j=2)
        sg = sb("sg", [P, 2, COLS], F32, mixing)
        rows = sb("rows", [16, 8, CH], F32, mixing)
        R_LI, R_LF, R_B, R_A, R_M, R_P, R_WK, R_EM = range(8)
        rtmp = sb("rtmp", [16, 2, CH], F32, mixing)
        gT = sb("gT", [NGATE, GROUP], F32, mixing)
        rcol = sb("rcol", [16, 3], F32, mixing)
        mlast = sb("mlast", [1, 2, 16], F32, mixing)
        diag = sb("diag", [16, 2, 16], F32, mixing)
        bc = sb("bc", [P, 2, 16], F32, mixing)
        cols = sb("cols", [P, 3, 16], F32, mixing)
        pdiag = gT[0:16].rearrange("p (h t) -> p h t", h=HEADS)
        mw = sb("mw", [P, 3 * COLS], F32, mixing)
        ew, arg, wk = (mw[:, k * COLS:(k + 1) * COLS].rearrange("p (h t) -> p h t", h=HEADS) for k in range(3))
        qw, sm = (sg[:, k, :].rearrange("p (h t) -> p h t", h=HEADS) for k in range(2))
        msk = mw[:, 0:2 * 448].rearrange("p (b l t) -> p b l t", b=2, l=7)
        ad_odd = sb("ad_odd", [P, HEADS, 64], F32, mixing)
        ad = (mw[:, 896:1152].rearrange("p (h t) -> p h t", h=HEADS), ad_odd)
        a2 = mw[0:64, 1152:1408].rearrange("p (h t) -> p h t", h=HEADS)
        head_g = sb("head_g", [P, D], F32, mixing)
        eb = head_g[:, 0:COLS].rearrange("p (b j t) -> p b j t", b=2, j=2)
        ekw = head_g[:, COLS:].rearrange("p (b j t) -> p b j t", b=2, j=2)
        bend = sb("bend", [P, 2, NCH], F32, mixing)
        qe = sb("qe", [P, 2, 2, CH], F32, mixing)
        kwT = sb("kwT", [P, 2 * CH], F32, mixing)
        mixing.close()
        later = ExitStack()
        h_hi = sb("h_hi", [P, KT, GROUP], F32R, later)
        h_lo = sb("h_lo", [P, KT, GROUP], F32R, later)
        mlp = ExitStack()
        hr = sb("hr", [P, 4, GROUP], F32, mlp)
        hsq = sb("hsq", [P, 2, GROUP], F32, mlp)
        fin_g = sb("fin_g", [P, D], F32, mlp)
        mlp.close()
        attn = ExitStack()
        pr = sb("pr", [P, 2, HEADS, MEM], F32, attn)
        prT = sb("prT", [P, HEADS, 2, GROUP], F32, attn)
        smax = sb("smax", [P, 2, HEADS], F32, attn)
        ssum = sb("ssum", [P, 2, HEADS], F32, attn)
        sinv = sb("sinv", [P, 2, HEADS], F32, attn)
        attn.close()
        later.close()

        bank = [ctx.enter_context(nc.psum_tensor(f"bank{i}", [P, 512], F32)) for i in range(4)]
        work = ctx.enter_context(nc.psum_tensor("work", [P, 4, 512], F32))

        mem_in = sem("mem_in")
        const_in = sem("const_in")
        ident_made = sem("ident_made")
        const_made = sem("const_made")
        gate_w_hi = sem("gate_w_hi")
        gate_w_lo = sem("gate_w_lo")
        x_in = sem("x_in")
        next_in = sem("next_in")
        pair_in = [sem(f"pair_in{i}") for i in range(PAIRS)]
        slab_hi = sem("slab_hi")
        slab_lo = sem("slab_lo")
        slab_used = sem("slab_used")
        bank_full = sem("bank_full")
        bank_free = sem("bank_free")
        act_step = sem("act_step")
        dve_step = sem("dve_step")
        pe_step = sem("pe_step")
        pool_step = sem("pool_step")
        norm_ss = sem("norm_ss")
        norm_var = sem("norm_var")
        norm_guess = sem("norm_guess")
        tok_ready = sem("tok_ready")
        tr_full = sem("tr_full")
        act_hi_ready = sem("act_hi_ready")
        act_lo_ready = sem("act_lo_ready")
        gates_full = sem("gates_full")
        gates_out = sem("gates_out")
        grow_full = sem("grow_full")
        grow_out = sem("grow_out")
        la_full = sem("la_full")
        la_abs = sem("la_abs")
        la_min = sem("la_min")
        la_log = sem("la_log")
        row_log = sem("row_log")
        row_scan = sem("row_scan")
        mlast_full = sem("mlast_full")
        mrow_ready = sem("mrow_ready")
        mcol_full = sem("mcol_full")
        row_p = sem("row_p")
        row_exp = sem("row_exp")
        diag_ready = sem("diag_ready")
        cols_full = sem("cols_full")
        cols_ready = sem("cols_ready")
        conv_done = sem("conv_done")
        conv_sig = sem("conv_sig")
        qk_ready = sem("qk_ready")
        og_scaled = sem("og_scaled")
        gr_sig = sem("gr_sig")
        pdiag_ready = sem("pdiag_ready")
        ps_full = sem("ps_full")
        m_arg = sem("m_arg")
        m_exp = sem("m_exp")
        m_in = sem("m_in")
        kt_full = sem("kt_full")
        wk_ready = sem("wk_ready")
        num_full = sem("num_full")
        num_ss = sem("num_ss")
        num_out = sem("num_out")
        c_full = sem("c_full")
        c_ready = sem("c_ready")
        gla_in = sem("gla_in")
        z_diff = sem("z_diff")
        z_exp = sem("z_exp")
        z_ready = sem("z_ready")
        ekw_ready = sem("ekw_ready")
        lvl_full = sem("lvl_full")
        lvl_masked = sem("lvl_masked")
        ad_ready = sem("ad_ready")
        side_full = sem("side_full")
        side_out = sem("side_out")
        o_full = sem("o_full")
        o_ss = sem("o_ss")
        o_out = sem("o_out")
        s_full = sem("s_full")
        s_ready = sem("s_ready")
        h_var = sem("h_var")
        h_guess = sem("h_guess")
        mixed = sem("mixed")
        sc_full = sem("sc_full")
        sc_max = sem("sc_max")
        sc_exp = sem("sc_exp")
        pr_ready = sem("pr_ready")
        prT_full = sem("prT_full")
        prT_out = sem("prT_out")
        sq_hi = sem("sq_hi")
        h_sq = sem("h_sq")
        h_ready = sem("h_ready")
        v_ones = sem("v_ones")
        carrier = sem("carrier")
        av_hi = sem("av_hi")
        head_g_in = sem("head_g_in")
        fin_g_in = sem("fin_g_in")
        kq_ready = sem("kq_ready")
        conv_first = sem("conv_first")
        stored = sem("stored")

        block = ctx.enter_context(nc.Block())

        def count(per_group, g, base, per_pass, hb):
            if isinstance(hb, int):
                return per_group * g + (per_pass * hb + base)
            return per_group * g + per_pass * hb + base

        def slab_no(g, s, hb=0):
            return count(GROUP_SLABS, g, PRO_SLABS + s, 4 * KT, hb)

        def use_no(g, u, hb=0):
            return count(GROUP_BANKS, g, PRO_BANKS + u, 16, hb)

        def read_out(eng, g, u, hb=0):
            eng.wait_ge(bank_free, use_no(g, u + 1, hb))

        def stand_alone(eng):
            eng.sem_inc(carrier, 1)

        def own_results(eng, signal, base, per):
            n, group = 0, None

            def mark(ins):
                nonlocal n
                ins.then_inc(signal, 1)
                n += 1

            def settle():
                eng.wait_ge(signal, n if group is None else base + per * group + n)

            def start_group(g):
                nonlocal n, group
                assert n == base, (n, base)
                n, group = 0, g

            def end_group():
                assert n == per, (n, per)

            return mark, settle, start_group, end_group

        @block.sync
        def _(sp):
            def load_pair(slot, seen, src):
                sp.dma_start(raw[:, slot], src).then_inc(pair_in[slot], 16)

            def pair_of(w, row, col):
                return w[row:row + 2 * P, col:col + COLS].rearrange("(k p) n -> p k n", p=P)

            small = [(norm_g[:, 0, :], A["mix_norm_g"]), (norm_g[:, 1, :], A["xattn_norm_g"]),
                     (norm_g[:, 2, :], A["mlp_norm_g"]), (conv_b[:, :], A["conv_b"]), (conv_w[:, :, :], A["conv_w"]),
                     (wa2[:, :], A["gla_wa2"]), (ba[:, :], A["gla_ba"]),
                     (wg_raw[:, :, RANK:],
                      A["w_in"][:, C_MI:C_MI + 2 * HEADS].rearrange("(k p) n -> p k n", p=P)),
                     (wg_raw[:, :, 0:RANK],
                      A["w_in"][:, C_GA:C_GA + RANK].rearrange("(k p) n -> p k n", p=P))]
            small += [(gate_b[c * HEADS:(c + 1) * HEADS, k:k + 1], A[name].rearrange("(h o) -> h o", o=1))
                      for c in range(NCH) for k, name in enumerate(("mlstm_i_b", "mlstm_f_b"))]
            assert len(small) == N_CONST

            q = 0
            for w, col in ((A["wk_x"], 0), (A["wk_x"], COLS), (A["wv_x"], 0), (A["wv_x"], COLS)):
                for kp in range(KT // 2):
                    if q >= PAIRS:
                        sp.wait_ge(slab_lo, 2 * (q - PAIRS + 1))
                    if q == 2 * PAIRS:
                        for dst, src in small:
                            sp.dma_start(dst, src).then_inc(const_in, 16)
                    load_pair(q % PAIRS, q, pair_of(w, kp * 2 * P, col))
                    q += 1

            fixed = [(A["w_in"], c) for c in (C_MQ, C_MK, C_MO, C_GR, C_MV, C_GQ, C_GV)]
            fixed += [(A["w_out"], 0), (A["w_out"], COLS), (A["wq_x"], 0), (A["wq_x"], COLS),
                      (A["wo_x"], 0), (A["wo_x"], COLS)]

            def load_slab_pair(n0, kp, src):
                sp.wait_ge(slab_lo, n0 + 2 * kp + 2 - 2 * PAIRS)
                load_pair(kp % PAIRS, None, src)

            with sp.Fori(0, NG) as g:
                for b, (w, col) in enumerate(fixed):
                    for kp in range(KT // 2):
                        load_slab_pair(slab_no(g, KT * b), kp, pair_of(w, kp * 2 * P, col))
                with sp.Fori(0, HB) as hb:
                    first = slab_no(g, KT * B_MLP, hb)
                    for b in range(2):
                        for kp in range(KT // 2):
                            load_slab_pair(first + KT * b, kp,
                                           A["w1"][kp * 2 * P:(kp + 1) * 2 * P, bass.ds(hb * D + b * COLS, COLS)]
                                           .rearrange("(k p) n -> p k n", p=P))
                    for b in range(2):
                        for kp in range(KT // 2):
                            load_slab_pair(first + KT * (2 + b), kp,
                                           A["w2"][bass.ds(hb * D + kp * 2 * P, 2 * P), b * COLS:(b + 1) * COLS]
                                           .rearrange("(k p) n -> p k n", p=P))
            for kp in range((LEAD + 1) // 2):
                load_slab_pair(slab_no(NG, 0), kp, pair_of(A["w_in"], kp * 2 * P, C_MQ))

        @block.gpsimd
        def _(pool):
            mark, settle, start_group, end_group = own_results(pool, pool_step, POOL_BASE, POOL_PER)

            def made(ins):
                mark(ins)
                settle()

            def select(view, pattern, base, cm, fill, op=ALU.is_ge):
                made(nc.gpsimd.affine_select(out=view, in_=view, compare_op=op, fill=fill, base=base,
                                             pattern=pattern, channel_multiplier=cm))

            made(nc.gpsimd.memset(ident[:], 0.0))
            nc.gpsimd.affine_select(out=ident[:], in_=ident[:], compare_op=ALU.not_equal, fill=1.0, base=0,
                                    pattern=[[-1, P]], channel_multiplier=1).then_inc(ident_made, 1)
            pool.wait_ge(ident_made, 1)
            made(nc.gpsimd.memset(ones16[:], 1.0))
            made(nc.gpsimd.memset(causal[:], 0.0))
            select(causal[:], [[1, P]], 0, -1, BIG)
            made(nc.gpsimd.memset(sel[:], 0.0))
            for a in range(2):
                first = RANK + HEADS * a
                select(sel[:, a], [[1, 28]], first - 12, -1, 1.0, ALU.not_equal)
                select(sel[:, a], [[0, 28]], -first, 1, 0.0)
                select(sel[:, a], [[0, 28]], first + HEADS - 1, -1, 0.0)
            tmp = qk[:, 0, 0:P]
            for lv in range(6):
                half = 32 >> lv
                nb = P // (2 * half)
                tv = tmp.rearrange("p (b r h) -> p b r h", r=2, h=half)
                made(nc.gpsimd.memset(tmp, 0.0))
                made(nc.gpsimd.memset(tv[:, :, 1, :], 1.0))
                select(tmp, [[-2 * half, nb], [0, 2 * half]], 0, 1, 0.0)
                select(tmp, [[2 * half, nb], [0, 2 * half]], half - 1, -1, 0.0)
                made(nc.gpsimd.tensor_copy(lvl_mask[0:64, lv, :], tmp[0:64, 0:64]))
                made(nc.gpsimd.tensor_copy(lvl_mask[64:128, lv, :], tmp[64:128, 64:128]))
            made(nc.gpsimd.tensor_copy(lvl_mask[0:64, 6, :], ident[0:64, 0:64]))
            made(nc.gpsimd.tensor_copy(lvl_mask[64:128, 6, :], ident[64:128, 64:128]))
            made(nc.gpsimd.memset(stC[:], 0.0))
            made(nc.gpsimd.memset(stS[:], 0.0))
            made(nc.gpsimd.memset(halo[:], 0.0))
            made(nc.gpsimd.memset(mrow[0:1, 1:NCH + 1, :], 0.0))
            nc.gpsimd.memset(mrow[0:1, 0, :], 0.0).then_inc(const_made, 1)

            pool.wait_ge(tok_ready, MEM // P)
            for i in range(NCH):
                pool.dma_start(xres[:, i, :], A["x"][i * P:(i + 1) * P, :]).then_inc(x_in, 16)
            with pool.Fori(0, NG) as g:
                start_group(g)
                pool.dma_start(head_g[:, 0:COLS], A["mlstm_norm_g"].partition_broadcast(P)).then_inc(head_g_in, 16)
                pool.dma_start(head_g[:, COLS:], A["gla_norm_g"].partition_broadcast(P)).then_inc(head_g_in, 16)
                pool.wait_ge(head_g_in, 32 * (g + 1))
                def gain_gates(half):
                    for i in range(NCH):
                        read_out(pool, g, 4 * (B_MO + half) + i)
                        v = tok[:, i, half * COLS:(half + 1) * COLS]
                        nc.gpsimd.tensor_tensor(v, v, head_g[:, half * COLS:(half + 1) * COLS],
                                                ALU.mult).then_inc(og_scaled, 1)

                def distances(c):
                    t0 = c * CH
                    if c == 0:
                        pool.wait_ge(gla_in, g + 1)
                    if c >= 2:
                        pool.wait_ge(lvl_full, 16 * g + 4 * (c - 1))
                        pool.wait_ge(side_full, 4 * g + c - 1)
                    for lv in range(LEVELS):
                        half = 64 >> lv
                        v = Z[:, c % 2, lv, :].rearrange("p (j b n) -> p j b n", j=2, n=2 * half)
                        src = decay[:, :, t0:t0 + CH].rearrange("p j (b n) -> p j b n", n=2 * half)
                        mid = src[:, :, :, half - 1:half].to_broadcast(list(src[:, :, :, 0:half].shape))
                        nc.gpsimd.tensor_tensor(v[:, :, :, 0:half], mid, src[:, :, :, 0:half], ALU.subtract)
                        ins = nc.gpsimd.tensor_tensor(v[:, :, :, half:], src[:, :, :, half:], mid, ALU.subtract)
                    ins.then_inc(z_diff, 1)

                def products(c):
                    t0 = c * CH
                    if c == 0:
                        read_out(pool, g, 4 * B_GQK + 3)
                    pool.wait_ge(z_exp, 4 * g + c + 1)
                    for lv in range(LEVELS):
                        half = 64 >> lv
                        v = Z[:, c % 2, lv, :].rearrange("p (j b r n) -> p j b r n", j=2, r=2, n=half)
                        for r, tile in ((0, 2), (1, 0)):
                            src = gqk[:, tile:tile + 2, t0:t0 + CH].rearrange(
                                "p j (b r n) -> p j b r n", r=2, n=half)[:, :, :, r, :]
                            ins = nc.gpsimd.tensor_tensor(v[:, :, :, r, :], v[:, :, :, r, :], src, ALU.mult)
                    ins.then_inc(z_ready, 1)

                def weigh_kq(c):
                    t0 = c * CH
                    pool.wait_ge(ekw_ready, 4 * g + c + 1)
                    if c >= 2:
                        pool.wait_ge(o_full, 4 * g + c - 1)
                    nc.gpsimd.tensor_tensor(ekw[:, c % 2], ekw[:, c % 2], gqk[:, 2:4, t0:t0 + CH], ALU.mult)
                    nc.gpsimd.tensor_tensor(qe[:, c % 2], eb[:, c % 2], gqk[:, 0:2, t0:t0 + CH],
                                            ALU.mult).then_inc(kq_ready, 1)

                gain_gates(0)
                distances(0)
                distances(1)
                gain_gates(1)
                for c in range(NCH):
                    if c >= 2:
                        distances(c)
                    products(c)
                    weigh_kq(c)
                pool.wait_ge(norm_ss, PRO_ROWS + 16 * g + 8)
                stand_alone(pool)
                pool.dma_start(fin_g[:], A["final_norm_g"].partition_broadcast(P)).then_inc(fin_g_in, 16)
                for i in range(NCH):
                    pool.dma_start(tok[:, i, :], A["x"][bass.ds((g + 1) % NG * GROUP + i * P, P), :])\
                        .then_inc(next_in, 16)
                pool.wait_ge(fin_g_in, 16 * (g + 1))
                for i in range(NCH):
                    pool.wait_ge(tok_ready, PRO_ROWS + 8 * g + 4 + i + 1)
                    mark(nc.gpsimd.tensor_tensor(xres[:, i, :], xres[:, i, :], fin_g[:], ALU.mult))
                    settle()
                    stand_alone(pool)
                    pool.dma_start(out[bass.ds(g * GROUP + i * P, P), :], xres[:, i, :]).then_inc(stored, 16)
                end_group()
                pool.wait_ge(stored, 16 * NCH * (g + 1))
                stand_alone(pool)
                for i in range(NCH):
                    pool.dma_start(xres[:, i, :], A["x"][bass.ds((g + 1) % NG * GROUP + i * P, P), :])\
                        .then_inc(x_in, 16)
            pool.wait_ge(x_in, 16 * NCH * (NG + 1))

        @block.scalar
        def _(act):
            mark, settle, start_group, end_group = own_results(act, act_step, ACT_BASE, ACT_PER)
            for dst, src in ((xres[:, 0, :], A["mem"][0:P, :]), (xres[:, 1, :], A["mem"][P:2 * P, :]),
                             (norm_g[:, 3, :], A["mem_norm_g"])):
                act.dma_start(dst, src).then_inc(mem_in, 16)

            nc.scalar.preload_act_table_set("natural_log_exp_and_others")

            def split_hi(slot, pair_slot, pair_count, use):
                if pair_count is not None:
                    act.wait_ge(pair_in[pair_slot], 16 * pair_count)
                if use is not None:
                    act.wait_ge(*use)
                nc.scalar.activation(w_hi[:, slot, :], raw[:, pair_slot, slot % 2, :], ACT.Copy).then_inc(slab_hi, 1)

            def split_pro(n):
                m = n - RING
                b, kt = divmod(m, KT)
                use = None if m < 0 else (slab_used, (KT - 1) * b + kt + 1) if kt < KT - 1 \
                    else (bank_full, (4, 8, 10, PRO_BANKS)[b])
                split_hi(n % RING, (n // 2) % PAIRS, n // 2 // PAIRS + 1 if n % 2 == 0 else None, use)

            def split(g, s, hb=0):
                n = s + LEAD
                b, kt = divmod(n - RING, KT)
                if kt < KT - 1:
                    use = (slab_used, count((KT - 1) * GROUP_SLABS // KT, g,
                                            (KT - 1) * (PRO_SLABS // KT + b) + kt + 1, 4 * (KT - 1), hb))
                else:
                    use = (bank_full, use_no(g, 4 * (b + 1) + (8 if b >= B_O else 0), hb))
                fills = count(GROUP_SLABS // 2 // PAIRS, g, PRO_SLABS // 2 // PAIRS + n // 2 // PAIRS + 1,
                              2 * KT // PAIRS, hb)
                split_hi(n % RING, (n // 2) % PAIRS, fills if n % 2 == 0 else None, use)

            def tile_hi(n, kt, width, gain, into=act_hi):
                act.wait_ge(tr_full, n + 1)
                src = work[:, kt % 4, 0:width]
                if gain is None:
                    ins = nc.scalar.activation(into[:, kt, 0:width], src, ACT.Copy)
                else:
                    ins = nc.scalar.activation(into[:, kt, 0:width], src, ACT.Copy,
                                               scale=norm_g[:, gain, kt:kt + 1])
                ins.then_inc(act_hi_ready, 1)

            def sum_squares(i, src=xres, squares=tok):
                nc.scalar.activation(squares[:, i, :], src[:, i, :], ACT.Square,
                                     accum_out=ss[:, i:i + 1]).then_inc(norm_ss, 1)

            def guess(n, count):
                act.wait_ge(norm_var, count)
                mark(nc.scalar.activation(lnv[:, 0:n], var[:, 0:n], ACT.Ln))
                settle()
                nc.scalar.activation(y0[:, 0:n], lnv[:, 0:n], ACT.Exp, scale=-0.5).then_inc(norm_guess, 1)

            act.wait_ge(mem_in, 16 * 3)
            for i in range(2):
                sum_squares(i)
            for n in range(LEAD):
                split_pro(n)
            guess(2, 1)
            for kt in range(KT):
                tile_hi(kt, kt, MEM, 3, h_hi)
            for b in range(4):
                for s in range(KT):
                    split_pro(KT * b + s + LEAD)
                    if b == 1 and s == 5:
                        act.wait_ge(const_in, 16 * N_CONST)
                        act.wait_ge(const_made, 1)
                        nc.scalar.activation(wg_hi[:], wg_raw[:], ACT.Copy).then_inc(gate_w_hi, 1)
                    if b == 1 and s == 2:
                        act.wait_ge(x_in, 16 * NCH)
                        for i in range(NCH):
                            sum_squares(i)
                        guess(NCH, 2)
                    if b == 2:
                        tile_hi(KT + s, s, GROUP, 0)
                for i in range(4 if b < 2 else 2):
                    u = 4 * b + i if b < 2 else 8 + 2 * (b - 2) + i
                    act.wait_ge(bank_full, u + 1)
                    if b < 2:
                        ins = nc.scalar.activation(memK[:, 4 * b + i, :], bank[i][:, 0:MEM], ACT.Copy)
                    else:
                        ins = nc.scalar.activation(memV[:, i, (b - 2) * COLS:(b - 1) * COLS],
                                                   bank[2 * (b - 2) + i][:], ACT.Copy)
                    ins.then_inc(bank_free, 1)
            split_pro(PRO_SLABS + LEAD)

            with act.Fori(0, NG) as g:
                start_group(g)

                def full(u):
                    act.wait_ge(bank_full, use_no(g, u + 1))

                def distance_exps(c):
                    act.wait_ge(z_diff, 4 * g + c + 1)
                    nc.scalar.activation(Z[:, c % 2], Z[:, c % 2], ACT.Exp, scale=1.0 / TAU).then_inc(z_exp, 1)

                def sum_exps(c):
                    t0 = c * CH
                    if c == 0:
                        act.wait_ge(og_scaled, 8 * g + 8)
                    if c >= 2:
                        act.wait_ge(s_ready, 4 * g + c - 1)
                    nc.scalar.activation(eb[:, c % 2], decay[:, :, t0:t0 + CH], ACT.Exp, scale=1.0 / TAU)
                    for j in range(2):
                        ins = nc.scalar.activation(ekw[:, c % 2, j, :], decay[:, j, t0:t0 + CH], ACT.Exp,
                                                   scale=-1.0 / TAU, bias=bend[:, j, c:c + 1])
                    ins.then_inc(ekw_ready, 1)

                junk = qk[:].rearrange("p (i r) n -> p i (r n)", r=2)

                def norm_tile(k, kt, into):
                    tile_hi(TRS * g + PRO_TR + 8 * (k + 1) + kt, kt, GROUP, k + 1, into)

                def norm_step(k, s, into):
                    if 1 <= s < 5:
                        norm_tile(k, s + 3, into)
                    if s in (5, 6, 9, 10):
                        sum_squares((5, 6, 9, 10).index(s), xres, tok if k == 0 else junk)
                    if s == 11:
                        guess(NCH, NORMS * g + PRO_NORMS + k + 1)

                nc.scalar.preload_act_table_set("natural_log_exp_and_others")

                for s in range(1, B_OUT * KT):
                    split(g, s)
                    b, r = divmod(s, KT)
                    if s == 8:
                        act.wait_ge(pool_step, POOL_PER * g + POOL_BASE)
                        act.wait_ge(gates_full, g + 1)
                        nc.scalar.activation(gT[:], work[0:NGATE, 0, :], ACT.Copy).then_inc(gates_out, 1)
                    if s == 11:
                        act.wait_ge(grow_full, g + 1)
                        nc.scalar.activation(rows[:, R_LI:R_LF + 1, :],
                                             work[0:16, 1, 0:2 * CH].rearrange("p (a t) -> p a t", a=2),
                                             ACT.Copy).then_inc(grow_out, 1)
                    if s == 13:
                        act.wait_ge(grow_out, g + 1)
                        nc.scalar.activation(rtmp[:, 0, :], rows[:, R_LF, :], ACT.Abs, bias=gate_b[:, 1:2])
                        act.wait_ge(la_min, g + 1)
                        for j in range(2):
                            ins = nc.scalar.activation(decay[:, j, :], work[:, 3 * (1 - j), :], ACT.Abs,
                                                       bias=ba[:, j:j + 1])
                        ins.then_inc(la_abs, 1)
                    if b in (1, 2) and r % 2 == 0:
                        k = (b - 1) * 4 + r // 2
                        read_out(act, g, k)
                        nc.scalar.activation(qk[:, k, :], ubuf[:, r // 2, CONV - 1:], ACT.Identity,
                                             scale=conv_w[:, CONV - 1, k:k + 1],
                                             bias=conv_b[:, k:k + 1]).then_inc(conv_first, 1)
                    if b in (1, 2) and r % 2 == 1:
                        k = (b - 1) * 4 + r // 2
                        act.wait_ge(conv_done, KT * g + k + 1)
                        if k >= 2:
                            act.wait_ge(qk_ready, KT * g + k - 1)
                        nc.scalar.activation(sg[:, k % 2, :], qk[:, k, :], ACT.Sigmoid).then_inc(conv_sig, 1)
                    if r == KT - 1:
                        for i in range(4):
                            full(4 * b + i)
                            if b in (B_MQ, B_MK):
                                k = 4 * b + i
                                if b == B_MK:
                                    act.wait_ge(conv_done, KT * g + i + 1)
                                nc.scalar.activation(ubuf[:, i, 3:], bank[i][:], ACT.Copy)\
                                    .then_inc(bank_free, 1)
                            elif b == B_MO:
                                nc.scalar.activation(tok[:, i, 0:COLS], bank[i][:], ACT.Sigmoid)\
                                    .then_inc(bank_free, 1)
                            elif b == B_GR:
                                if i == 0:
                                    act.wait_ge(qk_ready, KT * g + KT)
                                if i >= 2:
                                    read_out(act, g, 4 * B_GR + i - 2)
                                nc.scalar.activation(sg[:, i % 2, :], bank[i][:], ACT.Sigmoid).then_inc(gr_sig, 1)
                            elif b == B_MV:
                                nc.scalar.activation(vext[:, i, :, 0:HD],
                                                     bank[i][:].rearrange("p (h n) -> p h n", h=HEADS),
                                                     ACT.Copy).then_inc(bank_free, 1)
                            elif b == B_GQK:
                                nc.scalar.activation(gqk[:, i, :], bank[i][:], ACT.Copy,
                                                     scale=DK ** -0.5 if i < 2 else 1.0)\
                                    .then_inc(bank_free, 1)
                            elif b == B_GV:
                                nc.scalar.activation(gv[:, i, :], bank[i][:], ACT.Copy)\
                                    .then_inc(bank_free, 1)
                    if s == 32:
                        nc.scalar.preload_act_table_set("natural_log_exp_and_others")
                    if s == 24:
                        nc.scalar.preload_act_table_set("natural_log_exp_and_others")
                        act.wait_ge(la_abs, g + 1)
                        mark(nc.scalar.activation(rtmp[:, 0, :], rtmp[:, 0, :], ACT.Exp, scale=-1.0))
                        mark(nc.scalar.activation(decay[:], decay[:], ACT.Exp, scale=-1.0))
                        settle()
                        nc.scalar.activation(rtmp[:, 0, :], rtmp[:, 0, :], ACT.Ln, bias=1.0).then_inc(row_log, 1)
                        nc.scalar.activation(decay[:], decay[:], ACT.Ln, bias=1.0).then_inc(la_log, 1)
                    if s == 29:
                        act.wait_ge(row_p, g + 1)
                        nc.scalar.activation(rows[:, R_WK, :], rows[:, R_A, :], ACT.Exp, bias=rcol[:, 1:2])
                        nc.scalar.activation(rows[:, R_EM, :], rows[:, R_EM, :], ACT.Exp, scale=-1.0)
                        nc.scalar.activation(rcol[:, 2:3], rcol[:, 0:1], ACT.Exp,
                                             bias=rcol[:, 1:2]).then_inc(row_exp, 1)
                    if M_SLAB <= s < M_SLAB + 4 * NCH:
                        c, stage = divmod(s - M_SLAB, 4)
                        if stage == 0:
                            act.wait_ge(m_arg, 4 * g + c + 1)
                            nc.scalar.activation(arg, arg, ACT.Exp, scale=-1.0).then_inc(m_exp, 1)
                            for h in range(HEADS):
                                r16 = c * HEADS + h
                                ins = nc.scalar.activation(ew[:, h, :], work[:, 0, h * CH:(h + 1) * CH], ACT.Exp,
                                                           scale=-1.0, bias=bc[:, 1, r16:r16 + 1])
                            ins.then_inc(m_exp, 1)
                        if stage == 2:
                            act.wait_ge(num_out, 4 * g + c + 1)
                            for h in range(HEADS):
                                ins = nc.scalar.activation(
                                    ew[:, h, :], work[:, 2 + h // 2, 256 * (h % 2):256 * (h % 2) + HD], ACT.Square,
                                    accum_out=hss[:, 0, c, h:h + 1])
                            ins.then_inc(num_ss, 1)
                    if s in (33, 34):
                        distance_exps(s - 33)
                    if s in (41, 45):
                        sum_exps((s - 41) // 4)

                def head_guess(half):
                    act.wait_ge(h_var, 2 * g + half + 1)
                    mark(nc.scalar.activation(hln[:, half], hvar[:, half], ACT.Ln))
                    settle()
                    nc.scalar.activation(hy0[:, half], hln[:, half], ACT.Exp, scale=-0.5).then_inc(h_guess, 1)

                for c in range(NCH):
                    act.wait_ge(side_full, 4 * g + c + 1)
                    if c >= 1:
                        act.wait_ge(s_full, 4 * g + c)
                    nc.scalar.activation(kwT[:], work[:, 3, 256:512], ACT.Copy)
                    nc.scalar.activation(a2[:], work[0:64, 3, 0:256].rearrange("p (h t) -> p h t", h=HEADS),
                                         ACT.Copy).then_inc(side_out, 1)
                    if c + 2 < NCH:
                        distance_exps(c + 2)
                    act.wait_ge(o_out, 4 * g + c + 1)
                    for h in range(HEADS):
                        ins = nc.scalar.activation(qw[:, h, :], work[:, 2, h * HD:(h + 1) * HD], ACT.Square,
                                                   accum_out=hss[:, 1, c, h:h + 1])
                    ins.then_inc(o_ss, 1)
                    if c == 0:
                        head_guess(0)
                    if c + 2 < NCH:
                        sum_exps(c + 2)

                head_guess(1)
                for kt in range(KT):
                    tile_hi(TRS * g + PRO_TR + kt, kt, GROUP, None)
                for s in range(B_OUT * KT, B_Q * KT):
                    split(g, s)
                    if s - B_OUT * KT in EARLY:
                        norm_tile(0, EARLY.index(s - B_OUT * KT), h_hi)
                for s in range(B_Q * KT, B_O * KT):
                    split(g, s)
                    norm_step(0, s - B_Q * KT, h_hi)
                    if s % KT == KT - 1:
                        b = s // KT - B_Q
                        for i in range(4):
                            full(U_Q + 4 * b + i)
                            nc.scalar.activation(qk[:, 4 * b + i, :], bank[i][:], ACT.Copy,
                                                 scale=XHD ** -0.5).then_inc(bank_free, 1)
                for i in range(NCH):
                    act.wait_ge(sc_max, 4 * g + i + 1)
                    if i >= 2:
                        act.wait_ge(prT_full, 8 * g + 2 * (i - 1))
                    for h in range(HEADS):
                        ins = nc.scalar.activation(pr[:, i % 2, h, :],
                                                   work[:, 2 * (i % 2) + h // 2, 256 * (h % 2):256 * (h % 2) + MEM],
                                                   ACT.Exp, bias=smax[:, i % 2, h:h + 1],
                                                   scale=rs_attn[:, i:i + 1],
                                                   accum_out=ssum[:, i % 2, h:h + 1])
                        if h % 2 == 1:
                            ins.then_inc(sc_exp, 1)
                    for half in range(2):
                        act.wait_ge(prT_full, 8 * g + 2 * i + half + 1)
                        nc.scalar.activation(
                            prT[:, 2 * half:2 * half + 2, :, i * P:(i + 1) * P],
                            bank[2 * (i % 2) + half][:].rearrange("p (h m t) -> p h m t", h=2, m=2),
                            ACT.Copy).then_inc(prT_out, 1)
                for k in range(KT):
                    full(U_PV + k)
                    nc.scalar.activation(h_hi[:, k, :], bank[k % 4][:], ACT.Copy).then_inc(av_hi, 1)
                for s in range(B_O * KT, B_MLP * KT):
                    split(g, s)
                    if s - B_O * KT in EARLY:
                        norm_tile(1, EARLY.index(s - B_O * KT), act_hi)

                def mlp_pass(hb, first=False, last=False):
                    for s in range(4 * KT):
                        split(g, B_MLP * KT + s, hb)
                        b, r = divmod(s, KT)
                        if first:
                            norm_step(1, s, act_hi)
                        if b < 2 and r == KT - 1:
                            for i in range(4):
                                k = 4 * b + i
                                n = count(8 * HB, g, k, 8, hb)
                                act.wait_ge(bank_full, use_no(g, U_MLP + k + 1, hb))
                                if b == 1:
                                    act.wait_ge(h_ready, n - 3)
                                nc.scalar.activation(hr[:, i, :], bank[i][:], ACT.Relu)\
                                    .then_inc(bank_free, 1)
                                read_out(act, g, U_MLP + k, hb)
                                nc.scalar.activation(h_hi[:, k, :], hr[:, i, :], ACT.Square).then_inc(sq_hi, 1)
                        if not last:
                            continue
                        if s == 0:
                            act.wait_ge(next_in, 16 * NCH * (g + 1))
                        if s in (0, 2, 4, 6):
                            sum_squares(s // 2, tok, junk)
                        if s == 10:
                            guess(NCH, NORMS * g + PRO_NORMS + 3)
                        if 17 <= s < 17 + KT:
                            kt = s - 17
                            tile_hi(TRS * g + PRO_TR + 24 + kt, kt, GROUP, 0)

                mlp_pass(0, first=True)
                with act.Fori(1, HB - 1) as hb:
                    mlp_pass(hb)
                mlp_pass(HB - 1, last=True)
                for i in range(NCH):
                    read_out(act, g, GROUP_BANKS - 4 + i)
                    sum_squares(i)
                    if i == 1:
                        split(g, GROUP_SLABS)
                guess(NCH, NORMS * g + PRO_NORMS + 4)
                end_group()


        @block.vector
        def _(dve):
            mark, settle, start_group, end_group = own_results(dve, dve_step, DVE_BASE, DVE_PER)
            tt, ts, stt = nc.vector.tensor_tensor, nc.vector.tensor_scalar, nc.vector.scalar_tensor_tensor

            def link(ins):
                mark(ins)
                settle()

            def split_lo(n, slot, pair_slot):
                dve.wait_ge(slab_hi, n + 1)
                tt(w_lo[:, slot, :], raw[:, pair_slot, slot % 2, :], w_hi[:, slot, :].bitcast(F32),
                   ALU.subtract).then_inc(slab_lo, 1)

            def split_at(n):
                split_lo(n, n % RING, (n // 2) % PAIRS)

            def split(g, s, hb=0):
                n = s + LEAD
                split_lo(slab_no(g, n, hb), n % RING, (n // 2) % PAIRS)

            def tile_lo(count, kt, width, gain, hi_lo=(act_hi, act_lo)):
                dve.wait_ge(act_hi_ready, count + 1)
                src, hi, lo = work[:, kt % 4, 0:width], hi_lo[0][:, kt, 0:width].bitcast(F32), hi_lo[1][:, kt, 0:width]
                if gain is None:
                    tt(lo, src, hi, ALU.subtract).then_inc(act_lo_ready, 1)
                else:
                    stt(out=lo, in0=src, scalar=norm_g[:, gain, kt:kt + 1], in1=hi, op0=ALU.mult,
                        op1=ALU.subtract).then_inc(act_lo_ready, 1)

            def row_scales(n, ss_count, k_count, into=rstd):
                dve.wait_ge(norm_ss, ss_count)
                ts(var[:, 0:n], ss[:, 0:n], 1.0 / D, EPS, ALU.mult, ALU.add).then_inc(norm_var, 1)
                dve.wait_ge(norm_guess, k_count)
                link(stt(out=y1[:, 0:n], in0=y0[:, 0:n], scalar=-0.5, in1=y0[:, 0:n], op0=ALU.mult, op1=ALU.mult))
                link(tt(y1[:, 0:n], y1[:, 0:n], var[:, 0:n], ALU.mult))
                link(stt(out=into[:, 0:n], in0=y1[:, 0:n], scalar=1.5, in1=y0[:, 0:n], op0=ALU.add, op1=ALU.mult))

            def scale_row(i, dst, src):
                ts(dst[:, i, :], src[:, i, :], rstd[:, i:i + 1], None, ALU.mult).then_inc(tok_ready, 1)

            for n in range(LEAD):
                split_at(n)
            row_scales(2, 2, 1)
            for i in range(MEM // P):
                scale_row(i, tok, xres)
            for kt in range(KT):
                tile_lo(kt, kt, MEM, 3, (h_hi, h_lo))
            for n in range(LEAD, PRO_SLABS + LEAD + 1):
                split_at(n)
                s = n - LEAD
                if s == KT + 5:
                    dve.wait_ge(gate_w_hi, 1)
                    tt(wg_lo[:], wg_raw[:], wg_hi[:].bitcast(F32), ALU.subtract).then_inc(gate_w_lo, 1)
                if s == KT + 2:
                    row_scales(NCH, PRO_ROWS, 2)
                    for i in range(NCH):
                        scale_row(i, tok, xres)
                if 2 * KT <= s < 3 * KT:
                    tile_lo(KT + s % KT, s % KT, GROUP, 0)

            with dve.Fori(0, NG) as g:
                start_group(g)

                def full(u):
                    dve.wait_ge(bank_full, use_no(g, u + 1))

                def group_scales(k, into=rstd):
                    row_scales(NCH, PRO_ROWS + 4 * NORMS * g + 4 * (k + 1), NORMS * g + PRO_NORMS + k + 1, into)

                def norm_tile(k, kt, hi_lo):
                    tile_lo(TRS * g + PRO_TR + 8 * (k + 1) + kt, kt, GROUP, k + 1, hi_lo)

                def norm_step(k, s, hi_lo):
                    if 1 <= s < 5:
                        norm_tile(k, s + 3, hi_lo)
                    if s == 11:
                        group_scales(k, rs_attn if k == 0 else rs_mlp)
                        if k == 1:
                            link(tt(rs_mlp[:], rs_mlp[:], rs_mlp[:], ALU.mult))

                def add_block(b, u, col):
                    for i in range(4):
                        full(u + i)
                        v = xres[:, i, col:col + COLS]
                        tt(v, bank[i][:], v, ALU.add).then_inc(bank_free, 1)

                def level_sum(c, hd):
                    n = 16 * g + 4 * c + hd + 1
                    dve.wait_ge(lvl_full, n)
                    pl = work[:, hd % 2, 0:7 * 64].rearrange("p (l t) -> p l t", l=7)
                    tt(msk[:, hd % 2], pl, lvl_mask[:], ALU.mult).then_inc(lvl_masked, 1)
                    dve.wait_ge(lvl_masked, n)
                    if hd == 0 and c >= 2:
                        dve.wait_ge(o_full, 4 * g + c - 1)
                    nc.vector.tensor_reduce(ad[c % 2][:, hd, :], msk[:, hd % 2].rearrange("p l t -> p t l"), AX.X,
                                            ALU.add).then_inc(ad_ready, 1)

                def scale_heads(half):
                    y, z, h = hy0[:, half], hy1[:, half], hscale[:, half]
                    dve.wait_ge(h_guess, 2 * g + half + 1)
                    link(stt(out=z, in0=y, scalar=-0.5, in1=y, op0=ALU.mult, op1=ALU.mult))
                    link(tt(z, z, hvar[:, half], ALU.mult))
                    link(stt(out=h, in0=z, scalar=1.5, in1=y, op0=ALU.add, op1=ALU.mult))
                    if half == 0:
                        link(tt(h, h, hinv[:], ALU.mult))
                    v = tok[:, :, half * COLS:(half + 1) * COLS].rearrange("p c (h n) -> p c h n", h=HEADS)
                    tt(v, v, h.unsqueeze(3).to_broadcast([P, NCH, HEADS, HD]), ALU.mult).then_inc(mixed, 1)

                def weigh_p(c):
                    tt(pdiag[:], rows[:, R_P, :].unsqueeze(1).to_broadcast([16, HEADS, CH]),
                       ident[0:16, c * HEADS:(c + 1) * HEADS].unsqueeze(2).to_broadcast([16, HEADS, CH]),
                       ALU.mult).then_inc(pdiag_ready, 1)

                nc.vector.memset(vext[:, :, :, HD:HD + 1], 1.0).then_inc(v_ones, 1)
                for s in range(1, B_OUT * KT):
                    split(g, s)
                    b, r = divmod(s, KT)
                    if s == 13:
                        dve.wait_ge(grow_out, g + 1)
                        ts(rtmp[:, 1, :], rows[:, R_LF, :], gate_b[:, 1:2], 0.0, ALU.add, ALU.min)
                        dve.wait_ge(la_full, g + 1)
                        for j in range(2):
                            z = work[:, 3 * (1 - j), :]
                            ins = ts(zmin[:, j, :], z, ba[:, j:j + 1], 0.0, ALU.add, ALU.min)
                        ins.then_inc(la_min, 1)
                    if b in (1, 2):
                        k, i = (b - 1) * 4 + r // 2, r // 2
                        if r % 2 == 0:
                            read_out(dve, g, k)
                            mark(nc.vector.tensor_copy(ubuf[:, i, 0:CONV - 1], halo[:, k, :]))
                            acc = qk[:, k, :]
                            settle()
                            dve.wait_ge(conv_first, KT * g + k + 1)
                            for j in range(CONV - 1):
                                ins = stt(out=acc, in0=ubuf[:, i, j:j + GROUP], scalar=conv_w[:, j, k:k + 1],
                                          in1=acc, op0=ALU.mult, op1=ALU.add)
                                if j < CONV - 2:
                                    link(ins)
                            nc.vector.tensor_copy(halo[:, k, :], ubuf[:, i, GROUP:]).then_inc(conv_done, 1)
                        else:
                            dve.wait_ge(conv_sig, KT * g + k + 1)
                            acc = qk[:, k, :]
                            tt(acc, acc, sg[:, k % 2, :], ALU.mult).then_inc(qk_ready, 1)
                    if b == B_GR and r == KT - 1:
                        for i in range(4):
                            dve.wait_ge(gr_sig, 4 * g + i + 1)
                            tt(tok[:, i, COLS:], bank[i][:], sg[:, i % 2, :], ALU.mult)\
                                .then_inc(bank_free, 1)
                    if s == 25:
                        dve.wait_ge(row_log, g + 1)
                        link(tt(rows[:, R_LF, :], rtmp[:, 1, :], rtmp[:, 0, :], ALU.subtract))
                        link(nc.vector.tensor_tensor_scan(rows[:, R_B, :], rows[:, R_LF, :], rows[:, R_LF, :], 0.0,
                                                          ALU.add, ALU.bypass))
                        link(stt(out=rows[:, R_A, :], in0=rows[:, R_LI, :], scalar=gate_b[:, 0:1],
                                 in1=rows[:, R_B, :], op0=ALU.add, op1=ALU.subtract))
                        nc.vector.tensor_tensor_scan(rows[:, R_M, :], rows[:, R_A, :], rows[:, R_A, :],
                                                     -3e38, ALU.max, ALU.bypass).then_inc(row_scan, 1)
                    if s == 27:
                        dve.wait_ge(mlast_full, g + 1)
                        link(nc.vector.tensor_copy(mlast[:], work[0:1, 1, 0:32].rearrange("p (a r) -> p a r", a=2)))
                        for h in range(HEADS):
                            ins = nc.vector.tensor_tensor_scan(
                                mrow[0:1, 1:NCH + 1, h], mlast[0:1, 0, h:16:HEADS], mlast[0:1, 1, h:16:HEADS],
                                mrow[0:1, 0, h:h + 1], ALU.max, ALU.add)
                        ins.then_inc(mrow_ready, 1)
                    if s == 29:
                        dve.wait_ge(mcol_full, g + 1)
                        link(nc.vector.tensor_copy(rcol[:, 0:1], work[0:16, 2, 0:1]))
                        link(ts(rows[:, R_P, :], rows[:, R_M, :], rcol[:, 0:1], None, ALU.max))
                        tt(rows[:, R_EM, :], rows[:, R_B, :], rows[:, R_P, :], ALU.add)
                        ts(rcol[:, 1:2], rows[:, R_P, CH - 1:CH], -1.0, None, ALU.mult).then_inc(row_p, 1)
                    if s == 30:
                        dve.wait_ge(row_exp, g + 1)
                        ts(diag[:, 0, :], ident[0:16, 0:16], rcol[:, 2:3], None, ALU.mult)
                        ts(diag[:, 1, :], ident[0:16, 0:16], rcol[:, 0:1], None, ALU.mult).then_inc(diag_ready, 1)
                        nc.vector.tensor_copy(mrow[0:1, 0, :], mrow[0:1, NCH, :])
                        weigh_p(0)
                    if s == 32:
                        dve.wait_ge(cols_full, g + 1)
                        nc.vector.tensor_copy(bc[:], work[:, 1, 0:32].rearrange("p (a r) -> p a r", a=2))
                        nc.vector.tensor_copy(cols[:], work[:, 2, 0:48].rearrange("p (a r) -> p a r", a=3))\
                            .then_inc(cols_ready, 1)
                    if s == 26:
                        dve.wait_ge(la_log, g + 1)
                        link(tt(decay[:], zmin[:], decay[:], ALU.subtract))
                        for j in range(2):
                            for c in range(NCH):
                                v = decay[:, j, c * CH:(c + 1) * CH]
                                mark(nc.vector.tensor_tensor_scan(v, v, v, 0.0, ALU.add, ALU.bypass))
                        settle()
                        ts(bend[:], decay[:].rearrange("p j (c t) -> p j c t", c=NCH)[:, :, :, CH - 1], 1.0 / TAU, None,
                           ALU.mult).then_inc(gla_in, 1)
                    if M_SLAB <= s < M_SLAB + 4 * NCH:
                        c, stage = divmod(s - M_SLAB, 4)
                        t0 = c * CH
                        if stage == 0:
                            dve.wait_ge(ps_full, 4 * g + c + 1)
                            dve.wait_ge(cols_ready, g + 1)
                            for h in range(HEADS):
                                ins = stt(out=arg[:, h, :], in0=work[:, 0, h * CH:(h + 1) * CH],
                                          scalar=cols[:, 0, c * HEADS + h:c * HEADS + h + 1], in1=causal[:],
                                          op0=ALU.subtract, op1=ALU.add)
                            ins.then_inc(m_arg, 1)
                            dve.wait_ge(m_exp, 8 * g + 2 * c + 1)
                            stt(out=sm, in0=work[:, 1, :].rearrange("p (h t) -> p h t", h=HEADS),
                                scalar=HD ** -0.5, in1=arg, op0=ALU.mult, op1=ALU.mult)
                            dve.wait_ge(m_exp, 8 * g + 2 * c + 2)
                            stt(out=qw, in0=qk[:, 0:HEADS, t0:t0 + CH], scalar=HD ** -0.5, in1=ew,
                                op0=ALU.mult, op1=ALU.mult).then_inc(m_in, 1)
                        if stage == 1:
                            dve.wait_ge(kt_full, 4 * g + c + 1)
                            tt(wk[:], work[:, 0, :].rearrange("p (h d) -> p h d", h=HEADS),
                               cols[:, 1, c * HEADS:(c + 1) * HEADS].unsqueeze(2).to_broadcast([P, HEADS, HD]),
                               ALU.mult).then_inc(wk_ready, 1)
                            if c + 1 < NCH:
                                weigh_p(c + 1)
                        if stage == 2:
                            dve.wait_ge(num_full, 4 * g + c + 1)
                            dve.wait_ge(og_scaled, 8 * g + 4)
                            num = work[:, 2:4, :].rearrange("p b (h n) -> p (b h) n", h=2)
                            v = tok[:, c, 0:COLS].rearrange("p (h n) -> p h n", h=HEADS)
                            tt(v, num[:, :, 0:HD], v, ALU.mult)
                            nc.vector.tensor_copy(hden[:, c, :], num[:, :, HD]).then_inc(num_out, 1)
                        if stage == 3:
                            dve.wait_ge(c_full, 4 * g + c + 1)
                            upd = work[:, 0:2, :].rearrange("p b (h n) -> p (b h) n", h=2)
                            if c >= 1:
                                dve.wait_ge(c_ready, 4 * g + c)
                            for h in range(HEADS):
                                ins = stt(out=stC[:, h, :], in0=stC[:, h, :],
                                          scalar=bc[:, 0, c * HEADS + h:c * HEADS + h + 1],
                                          in1=upd[:, h, 0:HD + 1], op0=ALU.mult, op1=ALU.add)
                            ins.then_inc(c_ready, 1)
                    if s == G_SLAB:
                        dve.wait_ge(num_ss, 4 * g + 4)
                        level_sum(0, 0)
                        level_sum(0, 1)

                for c in range(NCH):
                    level_sum(c, 2)
                    level_sum(c, 3)
                    if c + 1 < NCH:
                        level_sum(c + 1, 0)
                        level_sum(c + 1, 1)
                    if c == 0:
                        dve.wait_ge(num_out, 4 * g + 4)
                        fl = [x.rearrange("p c h -> p (c h)") for x in (hden[:], hinv[:], hvar[:, 0], hss[:, 0])]
                        link(stt(out=fl[0], in0=fl[0], scalar=-1.0, in1=fl[0], op0=ALU.mult, op1=ALU.max))
                        link(tt(fl[0], fl[0], cols[:, 2, :], ALU.max))
                        link(nc.vector.reciprocal(fl[1], fl[0]))
                        link(tt(fl[2], fl[1], fl[1], ALU.mult))
                        link(tt(fl[2], fl[2], fl[3], ALU.mult))
                        ts(hvar[:, 0], hvar[:, 0], 1.0 / HD, EPS, ALU.mult, ALU.add).then_inc(h_var, 1)
                    dve.wait_ge(o_full, 4 * g + c + 1)
                    dve.wait_ge(og_scaled, 8 * g + 8)
                    v = tok[:, c, COLS:]
                    tt(v, work[:, 2, :], v, ALU.mult).then_inc(o_out, 1)
                    dve.wait_ge(s_full, 4 * g + c + 1)
                    if c >= 1:
                        dve.wait_ge(s_ready, 4 * g + c)
                    for j in range(2):
                        ins = stt(out=stS[:, j, :], in0=stS[:, j, :], scalar=eb[:, c % 2, j, CH - 1:CH],
                                  in1=work[:, 3, j * HD:(j + 1) * HD], op0=ALU.mult, op1=ALU.add)
                    ins.then_inc(s_ready, 1)
                    if c == 1:
                        scale_heads(0)
                dve.wait_ge(o_ss, 4 * g + 4)
                ts(hvar[:, 1], hss[:, 1], 1.0 / HD, EPS, ALU.mult, ALU.add).then_inc(h_var, 1)
                scale_heads(1)
                for kt in range(KT):
                    tile_lo(TRS * g + PRO_TR + kt, kt, GROUP, None)
                for s in range(B_OUT * KT, B_Q * KT):
                    split(g, s)
                    if s % KT == KT - 1:
                        b = s // KT - B_OUT
                        dve.wait_ge(x_in, 16 * NCH * (g + 1))
                        add_block(b, U_OUT + 4 * b, b * COLS)
                    if s - B_OUT * KT in EARLY:
                        norm_tile(0, EARLY.index(s - B_OUT * KT), (h_hi, h_lo))

                for s in range(B_Q * KT, B_O * KT):
                    split(g, s)
                    norm_step(0, s - B_Q * KT, (h_hi, h_lo))
                for i in range(NCH):
                    e = i % 2
                    sc = work[:, 2 * e:2 * e + 2, :].rearrange("p b (h m) -> p (b h) m", h=2)
                    dve.wait_ge(sc_full, 4 * g + i + 1)
                    link(nc.vector.tensor_reduce(smax[:, e, :], sc, AX.X, ALU.max))
                    ts(smax[:, e, :], smax[:, e, :], rs_attn[:, i:i + 1], -1.0, ALU.mult,
                       ALU.mult).then_inc(sc_max, 1)
                    for half in range(2):
                        hds = slice(2 * half, 2 * half + 2)
                        dve.wait_ge(sc_exp, 8 * g + 2 * i + half + 1)
                        link(nc.vector.reciprocal(sinv[:, e, hds], ssum[:, e, hds]))
                        tt(pr[:, e, hds], pr[:, e, hds], sinv[:, e, hds].unsqueeze(2).to_broadcast([P, 2, MEM]),
                           ALU.mult).then_inc(pr_ready, 1)
                for k in range(KT):
                    dve.wait_ge(av_hi, KT * g + k + 1)
                    tt(h_lo[:, k, :], bank[k % 4][:], h_hi[:, k, :].bitcast(F32),
                       ALU.subtract).then_inc(bank_free, 1)
                for s in range(B_O * KT, B_MLP * KT):
                    split(g, s)
                    if s % KT == KT - 1:
                        b = s // KT - B_O
                        add_block(b, U_O + 4 * b, b * COLS)
                    if s - B_O * KT in EARLY:
                        norm_tile(1, EARLY.index(s - B_O * KT), (act_hi, act_lo))

                def mlp_pass(hb, first=False, last=False):
                    for s in range(4 * KT):
                        split(g, B_MLP * KT + s, hb)
                        b, r = divmod(s, KT)
                        if first:
                            norm_step(1, s, (act_hi, act_lo))
                        if r == KT - 1 and b < 2:
                            for i in range(4):
                                k = 4 * b + i
                                n = count(8 * HB, g, k, 8, hb)
                                read_out(dve, g, U_MLP + k, hb)
                                tt(hsq[:, i % 2, :], hr[:, i, :], hr[:, i, :], ALU.mult).then_inc(h_sq, 1)
                                dve.wait_ge(h_sq, n + 1)
                                dve.wait_ge(sq_hi, n + 1)
                                tt(h_lo[:, k, :], hsq[:, i % 2, :], h_hi[:, k, :].bitcast(F32),
                                   ALU.subtract).then_inc(h_ready, 1)
                        if r == KT - 1 and b >= 2:
                            for i in range(4):
                                dve.wait_ge(bank_full, use_no(g, U_MLP + 4 * b + i + 1, hb))
                                v = xres[:, i, (b - 2) * COLS:(b - 1) * COLS]
                                stt(out=v, in0=bank[i][:], scalar=rs_mlp[:, i:i + 1], in1=v, op0=ALU.mult,
                                    op1=ALU.add).then_inc(bank_free, 1)
                        if not last:
                            continue
                        if s == 10:
                            group_scales(2)
                        if 11 <= s < 11 + NCH:
                            scale_row(s - 11, tok, tok)
                        if 17 <= s < 17 + KT:
                            kt = s - 17
                            tile_lo(TRS * g + PRO_TR + 24 + kt, kt, GROUP, 0)

                mlp_pass(0, first=True)
                with dve.Fori(1, HB - 1) as hb:
                    mlp_pass(hb)
                mlp_pass(HB - 1, last=True)
                split(g, GROUP_SLABS)
                group_scales(3)
                for i in range(NCH):
                    scale_row(i, xres, xres)
                end_group()

        @block.tensor
        def _(pe):
            mm, transpose = nc.tensor.matmul, nc.tensor.transpose
            mark, settle, start_group, end_group = own_results(pe, pe_step, 0, PE_PER)

            def slab(n, kt, major, prior, a_hi, a_lo, width=GROUP, tiles=4, bank0=0):
                slot = kt % RING
                pe.wait_ge(slab_lo, n + 1)
                for i in range(tiles):
                    if kt == 0 and prior is not None:
                        pe.wait_ge(bank_free, prior + i + 1)
                    dst = bank[bank0 + i][:, 0:width]
                    here = slice(i * P, (i + 1) * P)
                    if major == "feature":
                        terms = ((w_hi[:, slot, here], a_hi[:, kt, 0:width]),
                                 (w_hi[:, slot, here], a_lo[:, kt, 0:width]),
                                 (w_lo[:, slot, here], a_hi[:, kt, 0:width]))
                    else:
                        terms = ((a_hi[:, kt, here], w_hi[:, slot, :]),
                                 (a_hi[:, kt, here], w_lo[:, slot, :]),
                                 (a_lo[:, kt, here], w_hi[:, slot, :]))
                    for j, (left, right) in enumerate(terms):
                        ins = mm(dst, left, right, start=(kt == 0 and j == 0), stop=(kt == KT - 1 and j == 2))
                    if kt == KT - 1:
                        ins.then_inc(bank_full, 1)
                if kt < KT - 1:
                    ins.then_inc(slab_used, 1)

            def tiles_out(count0, ready, src_rows, tiles=range(KT), src=tok):
                for kt in tiles:
                    for signal, count in ready.get(kt, ()):
                        pe.wait_ge(signal, count)
                    if kt >= 4:
                        pe.wait_ge(act_lo_ready, count0 + kt - 3)
                    for i in range(src_rows):
                        ins = transpose(work[:, kt % 4, i * P:(i + 1) * P], src[:, i, kt * P:(kt + 1) * P], ident[:])
                    ins.then_inc(tr_full, 1)

            pe.wait_ge(ident_made, 1)
            tiles_out(0, {0: [(tok_ready, 2)]}, 2)
            for b in range(4):
                for kt in range(KT):
                    if b == 0:
                        pe.wait_ge(act_lo_ready, kt + 1)
                    if b == 2:
                        tiles_out(KT, {0: [(tok_ready, PRO_ROWS)]}, NCH, [kt])
                    if b < 2:
                        slab(KT * b + kt, kt, "feature", None if b == 0 else 0, h_hi, h_lo, MEM)
                    else:
                        slab(KT * b + kt, kt, "token", 4 + 2 * (b - 2), h_hi, h_lo, COLS, 2, 2 * (b - 2))
            pe.wait_ge(gate_w_lo, 1)

            with pe.Fori(0, NG) as g:
                start_group(g)

                def block_slab(s, major, u, tile_count=None, a_hi=act_hi, a_lo=act_lo):
                    kt = s % KT
                    if tile_count is not None:
                        pe.wait_ge(act_lo_ready, TRS * g + PRO_TR + tile_count + kt + 1)
                    slab(slab_no(g, s), kt, major, use_no(g, u - 4), a_hi, a_lo)

                def other_rows(ins):
                    mark(ins)
                    settle()
                    stand_alone(pe)

                def levels(c, hds):
                    pe.wait_ge(z_ready, 4 * g + c + 1)
                    t0 = c * CH
                    for hd in hds:
                        j, p0 = hd // 2, 64 * (hd % 2)
                        if 4 * c + hd >= 2:
                            pe.wait_ge(lvl_masked, 16 * g + 4 * c + hd - 1)
                        stand_alone(pe)
                        for q0 in (0, 64):
                            for lv in range(7):
                                dst = work[q0:q0 + 64, hd % 2, 64 * lv:64 * lv + 64]
                                if lv < 6:
                                    z = Z[p0:p0 + 64, c % 2, lv + 1, j * CH + q0:j * CH + q0 + 64]
                                    ins = mm(dst, z, z, start=True, stop=True)
                                else:
                                    here = slice(t0 + q0, t0 + q0 + 64)
                                    ins = mm(dst, gqk[p0:p0 + 64, 2 + j, here], gqk[p0:p0 + 64, j, here],
                                             start=True, stop=True)
                        ins.then_inc(lvl_full, 1)

                def side(c):
                    pe.wait_ge(kq_ready, 4 * g + c + 1)
                    if c >= 1:
                        pe.wait_ge(s_ready, 4 * g + c)
                    stand_alone(pe)
                    for hd in (0, 2, 1, 3):
                        j, p0 = hd // 2, 64 * (hd % 2)
                        ins = mm(work[0:64, 3, 64 * hd:64 * hd + 64], Z[p0:p0 + 64, c % 2, 0, j * CH:j * CH + 64],
                                 Z[p0:p0 + 64, c % 2, 0, j * CH + 64:j * CH + 128], start=True, stop=True)
                        if hd == 2:
                            other_rows(ins)
                    for j in range(2):
                        ins = transpose(work[:, 3, 256 + j * P:256 + (j + 1) * P], ekw[:, c % 2, j, :], ident[:])
                    ins.then_inc(side_full, 1)

                for s in range(B_OUT * KT):
                    b = s // KT
                    if s == 8:
                        for kt in range(KT):
                            for j, (left, right) in enumerate(((wg_hi, act_hi), (wg_lo, act_hi), (wg_hi, act_lo))):
                                ins = mm(work[0:NGATE, 0, :], left[:, kt, :], right[:, kt, :],
                                         start=(kt == 0 and j == 0), stop=(kt == KT - 1 and j == 2))
                        ins.then_inc(gates_full, 1)
                    if s == 11:
                        pe.wait_ge(gates_out, g + 1)
                        stand_alone(pe)
                        for a in range(2):
                            for c in range(NCH):
                                ins = mm(work[0:16, 1, a * CH:(a + 1) * CH],
                                         sel[:, a, HEADS * (NCH - 1 - c):HEADS * (NCH - 1 - c) + 16],
                                         gT[:, c * CH:(c + 1) * CH], start=(c == 0), stop=(c == NCH - 1))
                        ins.then_inc(grow_full, 1)
                        for j in range(2):
                            ins = mm(work[:, 3 * (1 - j), :], wa2[:, j * P:(j + 1) * P], gT[0:RANK, :],
                                     start=True, stop=True)
                        ins.then_inc(la_full, 1)
                    if s == 27:
                        pe.wait_ge(row_scan, g + 1)
                        stand_alone(pe)
                        for k, row in enumerate((R_M, R_B)):
                            ins = transpose(work[0:1, 1, 16 * k:16 * k + 16], rows[:, row, CH - 1:CH], ident[0:16, 0:16])
                        ins.then_inc(mlast_full, 1)
                    if s == 29:
                        pe.wait_ge(mrow_ready, g + 1)
                        stand_alone(pe)
                        mm(work[0:16, 2, 0:1], mrow[0:1, 0:NCH, :].rearrange("p c h -> p (c h)"), ones16[0:1, 0:1],
                           start=True, stop=True).then_inc(mcol_full, 1)
                    if s == 32:
                        pe.wait_ge(diag_ready, g + 1)
                        mm(work[:, 1, 0:32], ones16[:], diag[:].rearrange("p a r -> p (a r)"), start=True, stop=True)
                        for k, row in enumerate((R_A, R_WK, R_EM)):
                            ins = transpose(work[:, 2, 16 * k:16 * k + 16], rows[:, row, :], ident[0:16, 0:16])
                        ins.then_inc(cols_full, 1)
                    if M_SLAB <= s < M_SLAB + 4 * NCH:
                        c, stage = divmod(s - M_SLAB, 4)
                        t0 = c * CH
                        if stage == 0:
                            pe.wait_ge(pdiag_ready, 4 * g + c + 1)
                            pe.wait_ge(qk_ready, KT * g + KT)
                            if c == 0:
                                pe.wait_ge(cols_ready, g + 1)
                                pe.wait_ge(la_abs, g + 1)
                                pe.wait_ge(la_min, g + 1)
                            else:
                                pe.wait_ge(c_ready, 4 * g + c)
                            mm(work[:, 0, :], ones16[:], pdiag[:].rearrange("p h t -> p (h t)"), start=True, stop=True)
                            for h in range(HEADS):
                                ins = mm(work[:, 1, h * CH:(h + 1) * CH], qk[:, HEADS + h, t0:t0 + CH],
                                         qk[:, h, t0:t0 + CH], start=True, stop=True)
                            ins.then_inc(ps_full, 1)
                        if stage == 1:
                            pe.wait_ge(m_exp, 8 * g + 2 * c + 2)
                            for h in range(HEADS):
                                ins = transpose(work[:, 0, h * HD:(h + 1) * HD], qk[:, HEADS + h, t0:t0 + CH], ident[:])
                            ins.then_inc(kt_full, 1)
                        if stage == 2:
                            pe.wait_ge(m_in, 4 * g + c + 1)
                            read_out(pe, g, 4 * B_MV + 3)
                            pe.wait_ge(v_ones, g + 1)
                            if c >= 1:
                                pe.wait_ge(c_ready, 4 * g + c)
                                pe.wait_ge(num_out, 4 * g + c)
                                pe.wait_ge(num_ss, 4 * g + c)
                            for h in range(HEADS):
                                dst = work[:, 2 + h // 2, 256 * (h % 2):256 * (h % 2) + HD + 1]
                                mm(dst, qw[:, h, :], stC[:, h, :], start=True, stop=False)
                                ins = mm(dst, sm[:, h, :], vext[:, c, h, :], start=False, stop=True)
                            ins.then_inc(num_full, 1)
                        if stage == 3:
                            pe.wait_ge(wk_ready, 4 * g + c + 1)
                            for h in range(HEADS):
                                ins = mm(work[:, h // 2, 256 * (h % 2):256 * (h % 2) + HD + 1], wk[:, h, :],
                                         vext[:, c, h, :], start=True, stop=True)
                            ins.then_inc(c_full, 1)
                    if s == G_SLAB:
                        pe.wait_ge(c_ready, 4 * g + 4)
                        pe.wait_ge(num_out, 4 * g + 4)
                        pe.wait_ge(num_ss, 4 * g + 4)
                        levels(0, (0, 1))
                        side(0)
                    block_slab(s, "feature" if b in (B_MQ, B_MK, B_GQK) else "token", 4 * b, -KT if b == B_MQ else None)

                levels(0, (2, 3))
                read_out(pe, g, 4 * B_GV + 3)
                for c in range(NCH):
                    if c + 1 < NCH:
                        levels(c + 1, (0, 1))
                    pe.wait_ge(ad_ready, 16 * g + 4 * c + 4)
                    pe.wait_ge(side_out, 4 * g + c + 1)
                    if c >= 1:
                        pe.wait_ge(o_out, 4 * g + c)
                        pe.wait_ge(o_ss, 4 * g + c)
                    cut = [slice(hd * HD, (hd + 1) * HD) for hd in range(HEADS)]
                    for hd in (0, 2, 1, 3):
                        j, p0 = hd // 2, 64 * (hd % 2)
                        ins = mm(work[:, 2, cut[hd]], qe[p0:p0 + 64, c % 2, j, :], stS[p0:p0 + 64, j, :],
                                 start=(hd == 0), stop=False, skip_group_check=True)
                        if hd == 2:
                            other_rows(ins)
                    for hd in range(HEADS):
                        mm(work[0:64, 2, cut[hd]], ad[c % 2][0:64, hd, :], gv[0:64, c, cut[hd]], start=False, stop=True,
                           skip_group_check=True)
                        ins = mm(work[64:128, 2, cut[hd]], ad[c % 2][64:128, hd, :], gv[64:128, c, cut[hd]],
                                 start=False, stop=False, skip_group_check=True)
                    other_rows(ins)
                    for hd in range(HEADS):
                        ins = mm(work[64:128, 2, cut[hd]], a2[:, hd, :], gv[0:64, c, cut[hd]], start=False, stop=True,
                                 skip_group_check=True)
                    ins.then_inc(o_full, 1)
                    for hd in range(HEADS):
                        j, p0 = hd // 2, 64 * (hd % 2)
                        ins = mm(work[p0:p0 + 64, 3, j * HD:(j + 1) * HD], kwT[:, hd * DK:(hd + 1) * DK],
                                 gv[:, c, hd * HD:(hd + 1) * HD], start=True, stop=True)
                    ins.then_inc(s_full, 1)
                    if c + 1 < NCH:
                        levels(c + 1, (2, 3))
                        side(c + 1)

                tiles_out(TRS * g + PRO_TR, {0: [(lvl_masked, 16 * g + 16), (mixed, 2 * g + 1)],
                                             2: [(o_out, 4 * g + 4), (o_ss, 4 * g + 4)],
                                             3: [(s_ready, 4 * g + 4)],
                                             4: [(mixed, 2 * g + 2)]}, NCH)
                def norm_tile(k, kt, u):
                    tiles_out(TRS * g + PRO_TR + 8 * (k + 1),
                              {kt: [(bank_free, use_no(g, u + (4 if kt < 4 else 8)))]}, NCH, [kt], xres)

                for s in range(B_OUT * KT, B_Q * KT):
                    b = s // KT - B_OUT
                    if s - B_OUT * KT in EARLY:
                        norm_tile(0, EARLY.index(s - B_OUT * KT), U_OUT)
                    block_slab(s, "token", U_OUT + 4 * b, 0 if b == 0 else None)

                for s in range(B_Q * KT, B_O * KT):
                    b = s // KT - B_Q
                    if 1 <= s - B_Q * KT < 5:
                        norm_tile(0, s - B_Q * KT + 3, U_OUT)
                    block_slab(s, "feature", U_Q + 4 * b, 8 if b == 0 else None, h_hi, h_lo)

                def scores(i):
                    if i >= 2:
                        pe.wait_ge(sc_exp, 8 * g + 2 * i - 2)
                    for h in range(HEADS):
                        for k in range(2):
                            ins = mm(work[:, 2 * (i % 2) + h // 2, 256 * (h % 2):256 * (h % 2) + MEM],
                                     qk[:, 2 * h + k, i * P:(i + 1) * P], memK[:, 2 * h + k, :],
                                     start=(k == 0), stop=(k == 1))
                    ins.then_inc(sc_full, 1)

                def turn_probs(i):
                    for half in range(2):
                        pe.wait_ge(pr_ready, 8 * g + 2 * i + half + 1)
                        if i >= 2:
                            pe.wait_ge(prT_out, 8 * g + 2 * (i - 2) + half + 1)
                        for k in range(4):
                            ins = transpose(bank[2 * (i % 2) + half][:, k * P:(k + 1) * P],
                                            pr[:, i % 2, 2 * half + k // 2, (k % 2) * P:(k % 2 + 1) * P], ident[:])
                        ins.then_inc(prT_full, 1)

                read_out(pe, g, U_Q + 7)
                scores(0)
                scores(1)
                for i in range(NCH):
                    turn_probs(i)
                    if i + 2 < NCH:
                        scores(i + 2)
                pe.wait_ge(prT_out, 8 * g + 8)
                for k in range(KT):
                    pe.wait_ge(bank_free, use_no(g, U_PV + k - 4) + 1)
                    for m in range(2):
                        ins = mm(bank[k % 4][:], memV[:, m, k * P:(k + 1) * P], prT[:, k // 2, m, :],
                                 start=(m == 0), stop=(m == 1))
                    ins.then_inc(bank_full, 1)
                for s in range(B_O * KT, B_MLP * KT):
                    b = s // KT - B_O
                    if b == 0:
                        read_out(pe, g, U_PV + s % KT)
                    if s - B_O * KT in EARLY:
                        norm_tile(1, EARLY.index(s - B_O * KT), U_O)
                    block_slab(s, "token", U_O + 4 * b, None, h_hi, h_lo)

                def mlp_pass(hb, first=False, last=False):
                    for s in range(4 * KT):
                        b, kt = divmod(s, KT)
                        if first and 1 <= s < 5:
                            norm_tile(1, s + 3, U_O)
                        if first and b == 0:
                            pe.wait_ge(act_lo_ready, TRS * g + PRO_TR + 16 + kt + 1)
                        if last and b == 2:
                            tiles_out(TRS * g + PRO_TR + 24, {0: [(tok_ready, 8 * g + PRO_ROWS + 4)]}, NCH, [kt])
                        if b == 2:
                            pe.wait_ge(h_ready, count(8 * HB, g, kt + 1, 8, hb))
                        slab(slab_no(g, B_MLP * KT + s, hb), kt, "feature" if b < 2 else "token",
                             use_no(g, U_MLP + 4 * b - 4, hb),
                             act_hi if b < 2 else h_hi, act_lo if b < 2 else h_lo)

                mlp_pass(0, first=True)
                with pe.Fori(1, HB - 1) as hb:
                    mlp_pass(hb)
                mlp_pass(HB - 1, last=True)
                end_group()


N_CONST = 9 + 2 * NCH
ACT_BASE, ACT_PER = 2, 8
DVE_BASE, DVE_PER = 6, 76
PE_PER = 3 * NCH
POOL_BASE, POOL_PER = 53, 4

_INS = ['x', 'mem', 'mix_norm_g', 'w_in', 'conv_w', 'conv_b', 'mlstm_i_b', 'mlstm_f_b', 'mlstm_norm_g',
        'gla_wa2', 'gla_ba', 'gla_norm_g', 'w_out', 'xattn_norm_g', 'mem_norm_g', 'wq_x', 'wk_x', 'wv_x',
        'wo_x', 'mlp_norm_g', 'w1', 'w2', 'final_norm_g']


_BY_FEATURE = ('mix_norm_g', 'xattn_norm_g', 'mlp_norm_g', 'mem_norm_g', 'conv_w', 'conv_b', 'gla_ba')


def kernel(**inputs):
    import numpy as _np
    import concourse.bacc as _bacc
    from concourse import mybir as _mybir
    from concourse.bass_utils import run_bass_kernel_spmd as _run

    nc = _bacc.Bacc("TRN2", target_bir_lowering=False, num_devices=1)
    arrays, args = {}, {}
    for name in _INS:
        a = _np.ascontiguousarray(inputs[name])
        if name != 'final_norm_g':
            a = a.reshape(a.shape[1:])
        if name in _BY_FEATURE:
            a = _np.ascontiguousarray(_np.moveaxis(a.reshape(*a.shape[:-1], -1, 128), -1, 0))
        arrays[f"in_{name}_dram"] = a
        args[name] = nc.dram_tensor(f"in_{name}_dram", a.shape, _mybir.dt.from_np(a.dtype), kind="ExternalInput").ap()
    out = nc.dram_tensor("out_dram", (SEQ, D), _mybir.dt.float32, kind="ExternalOutput").ap()
    program(nc, args, out)
    r = _run(nc, [arrays], core_ids=[0])
    return r.results[0]["out_dram"].reshape(1, SEQ, D)
```
